# Optimizing a Trainium2 kernel written in Bass

```python
import jax, jax.numpy as jnp
from jax import lax
import numpy as np

D_MODEL = 1024
BATCH = 1
SEQ = 256
DEPTH = 1
DEC_BATCH = 8
DEC_SEQ = 8
PAST_LEN = 2048
PAGE_SIZE = 128

MIX_WIDTH = D_MODEL
LRU_WIDTH = MIX_WIDTH // 2
SGU_WIDTH = MIX_WIDTH - LRU_WIDTH
HEAD_DIM = 64
LRU_HEADS = LRU_WIDTH // HEAD_DIM
SGU_HEADS = SGU_WIDTH // HEAD_DIM
N_OUT_GROUPS = MIX_WIDTH // HEAD_DIM
CHUNK = 128
CONV_WIDTH = 4
LRU_C = 8.0
IN_COLS = 2 * LRU_WIDTH + 2 * SGU_WIDTH
N_EXPERTS = 64
TOP_K = 8
EXPERT_DIM = D_MODEL // 4
SHARED_DIM = D_MODEL // 4
ROUTED_SCALE = 2.5
EPS = 1e-6

kernel_name = 'hymba_style_rglru_sgu_moe_adaln_step'

def _rmsnorm(x, g):
    xf = x.astype(jnp.float32)
    y = xf * lax.rsqrt(jnp.mean(xf * xf, axis=-1, keepdims=True) + EPS)
    return (y * g.astype(jnp.float32)).astype(x.dtype)

def _group_rmsnorm(x, g, n_groups):
    shp = x.shape
    xf = x.astype(jnp.float32).reshape(shp[:-1] + (n_groups, shp[-1] // n_groups))
    y = xf * lax.rsqrt(jnp.mean(xf * xf, axis=-1, keepdims=True) + EPS)
    return (y.reshape(shp) * g.astype(jnp.float32)).astype(x.dtype)

def _modulations(c, ada_w, ada_b):
    mod = jax.nn.silu(c) @ ada_w + ada_b
    return jnp.split(mod[:, None, :], 6, axis=-1)

def _causal_conv(x, buf, w, b):
    T = x.shape[1]
    xp = jnp.concatenate([buf.astype(x.dtype), x], axis=1)
    y = b
    for k in range(CONV_WIDTH):
        y = y + w[k] * xp[:, k:k + T]
    return y, xp[:, -(CONV_WIDTH - 1):]

def _rg_lru(x, h0, wr, br, wi, bi, lam):
    B, T, _ = x.shape
    xh = x.reshape(B, T, LRU_HEADS, HEAD_DIM)
    r = jax.nn.sigmoid(jnp.einsum('bthi,hij->bthj', xh, wr).reshape(B, T, LRU_WIDTH) + br)
    i = jax.nn.sigmoid(jnp.einsum('bthi,hij->bthj', xh, wi).reshape(B, T, LRU_WIDTH) + bi)
    log_a = -LRU_C * r.astype(jnp.float32) * jax.nn.softplus(-lam.astype(jnp.float32))
    a = jnp.exp(log_a)
    u = jnp.sqrt(-jnp.expm1(2.0 * log_a)) * (i * x).astype(jnp.float32)
    u = u.at[:, 0].add(a[:, 0] * h0.astype(jnp.float32))

    def combine(left, right):
        a1, b1 = left
        a2, b2 = right
        return a1 * a2, a2 * b1 + b2

    _, h = lax.associative_scan(combine, (a, u), axis=1)
    h = h.astype(x.dtype)
    return h, h[:, -1]

def _spatial_gate(u, v, ws, bs):
    B, T, _ = v.shape
    L = min(T, CHUNK)
    n = T // L
    mask = jnp.tril(jnp.ones((L, L), dtype=bool))
    w = jnp.where(mask, ws[:, :L, :L], jnp.zeros((), ws.dtype))
    vc = v.reshape(B, n, L, SGU_HEADS, HEAD_DIM)
    s = jnp.einsum('gpq,bnqgd->bnpgd', w, vc) + bs[:, :L].T[None, None, :, :, None]
    return u * s.reshape(B, T, SGU_WIDTH)

def _mixer(xn, h0, conv_buf, l, p):
    proj = xn @ p['w_in'][l]
    xa, ga, pu, pv = jnp.split(proj, [LRU_WIDTH, 2 * LRU_WIDTH, 2 * LRU_WIDTH + SGU_WIDTH], axis=-1)
    xc, new_buf = _causal_conv(xa, conv_buf, p['conv_w'][l], p['conv_b'][l])
    h, h_last = _rg_lru(xc, h0, p['gate_r_w'][l], p['gate_r_b'][l], p['gate_i_w'][l], p['gate_i_b'][l], p['lru_lambda'][l])
    ya = h * jax.nn.gelu(ga)
    u = jax.nn.gelu(pu)
    v = _rmsnorm(jax.nn.gelu(pv), p['sgu_norm_g'][l])
    yb = _spatial_gate(u, v, p['sgu_w'][l], p['sgu_b'][l])
    y = _group_rmsnorm(jnp.concatenate([ya, yb], axis=-1), p['out_norm_g'][l], N_OUT_GROUPS)
    return y @ p['w_out'][l], h_last, new_buf, v

def _moe(xn, l, p):
    B, T, D = xn.shape
    x = xn.reshape(B * T, D)
    scores = jax.nn.sigmoid((x @ p['router_w'][l]).astype(jnp.float32))
    _, idx = lax.top_k(scores + p['router_bias'][l].astype(jnp.float32), TOP_K)
    sel = jnp.take_along_axis(scores, idx, axis=-1)
    wsel = sel / jnp.sum(sel, axis=-1, keepdims=True) * ROUTED_SCALE
    gates = jnp.sum(jax.nn.one_hot(idx, N_EXPERTS, dtype=jnp.float32) * wsel[..., None], axis=1).astype(x.dtype)
    hid = jax.nn.silu(jnp.einsum('nd,edf->nef', x, p['exp_w_gate'][l])) * jnp.einsum('nd,edf->nef', x, p['exp_w_up'][l])
    routed = jnp.einsum('nef,efd->nd', hid * gates[..., None], p['exp_w_down'][l])
    shared = (jax.nn.silu(x @ p['shared_w_gate'][l]) * (x @ p['shared_w_up'][l])) @ p['shared_w_down'][l]
    return (routed + shared).reshape(B, T, D)

def _trunk(x, c, h_state, conv_state, p):
    hs, bufs, vs = [], [], []
    for l in range(DEPTH):
        sh_m, sc_m, g_m, sh_f, sc_f, g_f = _modulations(c, p['ada_w'][l], p['ada_b'][l])
        xn = _rmsnorm(x, p['norm_mix_g'][l]) * (1.0 + sc_m) + sh_m
        y, h_last, buf, v = _mixer(xn, h_state[l], conv_state[l], l, p)
        x = x + g_m * y
        xn = _rmsnorm(x, p['norm_ffn_g'][l]) * (1.0 + sc_f) + sh_f
        x = x + g_f * _moe(xn, l, p)
        hs.append(h_last)
        bufs.append(buf)
        vs.append(v)
    return _rmsnorm(x, p['final_norm_g']), jnp.stack(hs), jnp.stack(bufs), vs

def setup_inputs(seed: int = 0) -> dict:
    key = jax.random.key(seed)
    ks = jax.random.split(key, 40)
    nrm = lambda k, shape, s: jax.random.normal(k, shape, jnp.float32) * s
    gain = lambda k, shape: 1.0 + 0.02 * jax.random.normal(k, shape, jnp.float32)
    a0 = jax.random.uniform(ks[0], (DEPTH, LRU_WIDTH), jnp.float32, minval=0.9, maxval=0.999)
    a_base = a0 ** (1.0 / LRU_C)
    return {
        'x_prompt': nrm(ks[1], (BATCH, SEQ, D_MODEL), 1.0),
        'x_sample': nrm(ks[2], (DEC_BATCH, DEC_SEQ, D_MODEL), 1.0),
        'c_prompt': nrm(ks[3], (BATCH, D_MODEL), 1.0),
        'c_sample': nrm(ks[4], (DEC_BATCH, D_MODEL), 1.0),
        'state_lru_h': nrm(ks[5], (DEPTH, DEC_BATCH, LRU_WIDTH), 1.0),
        'state_conv': nrm(ks[6], (DEPTH, DEC_BATCH, CONV_WIDTH - 1, LRU_WIDTH), 1.0),
        'ada_w': nrm(ks[7], (DEPTH, D_MODEL, 6 * D_MODEL), 0.3 * D_MODEL ** -0.5),
        'ada_b': nrm(ks[8], (DEPTH, 6 * D_MODEL), 0.02),
        'norm_mix_g': gain(ks[9], (DEPTH, D_MODEL)),
        'norm_ffn_g': gain(ks[10], (DEPTH, D_MODEL)),
        'w_in': nrm(ks[11], (DEPTH, D_MODEL, IN_COLS), D_MODEL ** -0.5),
        'conv_w': nrm(ks[12], (DEPTH, CONV_WIDTH, LRU_WIDTH), CONV_WIDTH ** -0.5),
        'conv_b': nrm(ks[13], (DEPTH, LRU_WIDTH), 0.02),
        'gate_r_w': nrm(ks[14], (DEPTH, LRU_HEADS, HEAD_DIM, HEAD_DIM), HEAD_DIM ** -0.5),
        'gate_r_b': nrm(ks[15], (DEPTH, LRU_WIDTH), 0.02),
        'gate_i_w': nrm(ks[16], (DEPTH, LRU_HEADS, HEAD_DIM, HEAD_DIM), HEAD_DIM ** -0.5),
        'gate_i_b': nrm(ks[17], (DEPTH, LRU_WIDTH), 0.02),
        'lru_lambda': jnp.log(a_base) - jnp.log1p(-a_base),
        'sgu_norm_g': gain(ks[18], (DEPTH, SGU_WIDTH)),
        'sgu_w': nrm(ks[19], (DEPTH, SGU_HEADS, CHUNK, CHUNK), 0.5 * CHUNK ** -0.5),
        'sgu_b': gain(ks[20], (DEPTH, SGU_HEADS, CHUNK)),
        'out_norm_g': gain(ks[21], (DEPTH, MIX_WIDTH)),
        'w_out': nrm(ks[22], (DEPTH, MIX_WIDTH, D_MODEL), MIX_WIDTH ** -0.5),
        'router_w': nrm(ks[23], (DEPTH, D_MODEL, N_EXPERTS), D_MODEL ** -0.5),
        'router_bias': nrm(ks[24], (DEPTH, N_EXPERTS), 0.01),
        'exp_w_gate': nrm(ks[25], (DEPTH, N_EXPERTS, D_MODEL, EXPERT_DIM), D_MODEL ** -0.5),
        'exp_w_up': nrm(ks[26], (DEPTH, N_EXPERTS, D_MODEL, EXPERT_DIM), D_MODEL ** -0.5),
        'exp_w_down': nrm(ks[27], (DEPTH, N_EXPERTS, EXPERT_DIM, D_MODEL), EXPERT_DIM ** -0.5),
        'shared_w_gate': nrm(ks[28], (DEPTH, D_MODEL, SHARED_DIM), D_MODEL ** -0.5),
        'shared_w_up': nrm(ks[29], (DEPTH, D_MODEL, SHARED_DIM), D_MODEL ** -0.5),
        'shared_w_down': nrm(ks[30], (DEPTH, SHARED_DIM, D_MODEL), SHARED_DIM ** -0.5),
        'final_norm_g': gain(ks[31], (D_MODEL,)),
    }

def reference(x_prompt, x_sample, c_prompt, c_sample, state_lru_h, state_conv, ada_w, ada_b, norm_mix_g, norm_ffn_g, w_in, conv_w, conv_b, gate_r_w, gate_r_b, gate_i_w, gate_i_b, lru_lambda, sgu_norm_g, sgu_w, sgu_b, out_norm_g, w_out, router_w, router_bias, exp_w_gate, exp_w_up, exp_w_down, shared_w_gate, shared_w_up, shared_w_down, final_norm_g):
    p = dict(ada_w=ada_w, ada_b=ada_b, norm_mix_g=norm_mix_g, norm_ffn_g=norm_ffn_g, w_in=w_in, conv_w=conv_w, conv_b=conv_b,
             gate_r_w=gate_r_w, gate_r_b=gate_r_b, gate_i_w=gate_i_w, gate_i_b=gate_i_b, lru_lambda=lru_lambda,
             sgu_norm_g=sgu_norm_g, sgu_w=sgu_w, sgu_b=sgu_b, out_norm_g=out_norm_g, w_out=w_out,
             router_w=router_w, router_bias=router_bias, exp_w_gate=exp_w_gate, exp_w_up=exp_w_up, exp_w_down=exp_w_down,
             shared_w_gate=shared_w_gate, shared_w_up=shared_w_up, shared_w_down=shared_w_down, final_norm_g=final_norm_g)
    nb = x_prompt.shape[0]
    h0_prompt = jnp.zeros((DEPTH, nb, LRU_WIDTH), x_prompt.dtype)
    conv0_prompt = jnp.zeros((DEPTH, nb, CONV_WIDTH - 1, LRU_WIDTH), x_prompt.dtype)
    y_prompt, new_lru_h_prompt, new_conv_prompt, _ = _trunk(x_prompt, c_prompt, h0_prompt, conv0_prompt, p)
    y_sample, new_lru_h_sample, new_conv_sample, v_sample = _trunk(x_sample, c_sample, state_lru_h, state_conv, p)
    new_sgu_v_sample = jnp.stack(v_sample)
    return (y_prompt, y_sample, new_lru_h_prompt, new_conv_prompt, new_lru_h_sample, new_conv_sample, new_sgu_v_sample)


_drawn_inputs = setup_inputs


def setup_inputs(seed=0):
    import zlib

    import numpy as np

    out = dict(_drawn_inputs(seed))
    spreads = {}
    factors = {'norm_mix_g': 2.814,
     'norm_ffn_g': 4.174,
     'gate_r_b': 8.0,
     'gate_i_b': 7.986,
     'sgu_norm_g': 2.998,
     'sgu_b': 8.0,
     'out_norm_g': 8.0,
     'final_norm_g': 2.889}
    for name, (base, spread) in spreads.items():
        noise = np.random.default_rng([zlib.crc32(name.encode()), seed]).standard_normal(out[name].shape)
        drawn = base * np.exp(spread * noise) if base else spread * noise
        out[name] = __import__('jax').numpy.asarray(drawn.astype(out[name].dtype))
    for name, factor in factors.items():
        out[name] = (out[name] * factor).astype(out[name].dtype)
    return out
```

```python
from contextlib import ExitStack

import concourse.bass as bass
from concourse import mybir

F32 = mybir.dt.float32
U32 = mybir.dt.uint32
BF16 = mybir.dt.bfloat16
I32 = mybir.dt.int32
ALU = mybir.AluOpType
ACT = mybir.ActivationFunctionType
AX = mybir.AxisListType.X

P = 128
D = 1024
KT = D // P
NPR = 256
NB, NT = 8, 8
T = NPR + NB * NT
TILES = [(0, 128), (128, 128), (256, 64)]
W = 512
CW = 4
CT = W // P
NE = 64
FE = 256
NSEQ = 9
EPS = 1e-6
HALF = D // 2
OOB = 2 * D
SLOTS = 4
U = 8
ROUND = 128
ROUNDS = -(-T // ROUND)
SEG = NPR + CW - 1
SS = NT + CW - 1


def build(nc, io):
    with ExitStack() as ctx:
        ctx.enter_context(nc.allow_non_contiguous_dma(reason="small transposed bias rows"))

        def sb(name, shape, dt=F32):
            return ctx.enter_context(nc.sbuf_tensor(name, shape, dt))

        def sem(name):
            return ctx.enter_context(nc.semaphore(name))

        xn_rows = nc.dram_tensor("xn_rows", [T, D], F32).ap()
        acc_rows = [nc.dram_tensor(f"acc_rows{b}", [2 * T, HALF], F32).ap() for b in range(2)]
        mod_rows = nc.dram_tensor("mod_rows", [NSEQ, 6 * D], F32).ap()
        xn_half = xn_rows.rearrange("t (h n) -> (t h) n", h=2)

        gu = [sb(f"gu{s}", [P, KT, 512]) for s in range(SLOTS)]
        dn = sb("dn", [P, SLOTS, 2 * D])
        x = sb("x", [P, 3, D])
        xn = sb("xn", [P, 3, D])
        xT = sb("xT", [P, KT, T])
        mb = sb("mb", [P, 2, 2, D])
        gmod = sb("gmod", [P, 2, D])
        gn = sb("gn", [P, D])
        sh = sb("sh", [P, 3, D])
        et = sb("et", [P, 7424])
        ident = sb("ident", [P, P])
        ones = sb("ones", [P, P])
        upper = sb("upper", [P, P])
        blk = sb("blk", [P, P])
        cT = sb("cT", [P, KT, 32])
        chT = sb("chT", [P, CT, 41])
        small = sb("small", [P, 64])
        wrt = sb("wrt", [P, KT, NE])
        rbias = sb("rbias", [P, NE])
        iota_s = sb("iota_s", [P, 256])
        tokc = sb("tokc", [P, 3])
        halfc = sb("halfc", [P, 1])
        cnt_i = sb("cnt_i", [P, NE + 1], I32)
        idx = sb("idx", [P, U, 2], U32)
        pick_out = sb("pick_out", [P, U, 2, 2])
        hc = sb("hc", [P, CT, 36])

        dnf = dn[:, :, :].rearrange("p s n -> p (s n)")

        def lru(n):
            return dnf[:, n * 1280:(n + 1) * 1280].rearrange("p (c t) -> p c t", c=CT)
        xc, rr, aa, ii, dd, ga = (lru(n) for n in range(6))
        chrow = dnf[:, 7680:8192]
        o = [0]

        def part(n):
            o[0] += n
            return et[:, o[0] - n:o[0]]
        xap = part(CT * (SEG + NB * SS)).rearrange("p (c t) -> p c t", c=CT)
        wnat = part(1024).rearrange("p (g q) -> p g q", g=8)
        wT = part(1024).rearrange("p (g q) -> p g q", g=8)
        wsn = part(512).rearrange("p (g q) -> p g q", g=8)
        wsT = part(512).rearrange("p (g q) -> p g q", g=8)
        vg_row = part(512)
        og_row = part(512)
        mods = part(12 * P).rearrange("p (j n) -> p j n", j=12)
        bsT = part(8)
        bsS = part(8)
        assert o[0] <= 7424
        shf = sh[:, :, :].rearrange("p t n -> p (t n)")
        wr = shf[:, 0:512].rearrange("p (c j) -> p c j", c=CT)
        wi = shf[:, 512:1024].rearrange("p (c j) -> p c j", c=CT)
        adab = shf[:, 1024:2560].rearrange("p (j n) -> p j n", j=12)
        hrow = shf[:, 2560:3072]
        xnf = xn[:, :, :].rearrange("p t n -> p (t n)")
        us = xnf[:, 0:1536].rearrange("p (t n) -> p t n", t=3)
        vv = xnf[:, 1536:3072].rearrange("p (t n) -> p t n", t=3)
        crow = gmod[0:32, 0, :]
        o[0] = 0
        xg = part(2048).rearrange("p (b s n) -> p b s n", b=2, s=2)
        xt = part(1024).rearrange("p (s k h n) -> p s k h n", s=2, k=4, h=2)
        sg = part(512)
        up = part(512)
        hid = part(512).rearrange("p (s j f) -> p s j f", s=2, j=2)
        hT = part(256).rearrange("p (s j n) -> p s j n", s=2, j=2)
        sel = part(384).bitcast(BF16).rearrange("p (t n) -> p t n", t=3)
        yo = part(2048).rearrange("p (a s n) -> p a s n", a=2, s=2)
        shid = et[:, o[0] - 768:o[0] - 512]
        shT = et[:, o[0] - 512:o[0] - 256].rearrange("p (j n) -> p j n", j=2)
        sgs = et[:, o[0] - 256:o[0]]
        sqy = et[:, 3072:4096]
        assert o[0] <= 7424
        mbf = mb[:, :, :, :].rearrange("p a b n -> p (a b n)")
        score = mbf[:, 0:192].rearrange("p (t e) -> p t e", t=3)
        biased = mbf[:, 192:384].rearrange("p (t e) -> p t e", t=3)
        rest = mbf[:, 384:576].rearrange("p (t e) -> p t e", t=3)
        mask = mbf[:, 576:768].rearrange("p (t e) -> p t e", t=3)
        pos = mbf[:, 768:960].rearrange("p (t e) -> p t e", t=3)
        top = mbf[:, 960:984].rearrange("p (t e) -> p t e", t=3)
        tg = mbf[:, 1440:1440 + 576].bitcast(BF16).rearrange("p (t e c m) -> p t e c m", t=3, c=2, m=3)
        gpart = mbf[:, 2048:2240].rearrange("p (t e) -> p t e", t=3)
        cmax = mbf[:, 1400:1401]
        rsc = mbf[:, 1408:1420]

        bank = [ctx.enter_context(nc.psum_tensor(f"bank{b}", [P, 512], F32)) for b in range(8)]

        names = """v_out consts consts_v crow_zero blk_zero ld_c ld_x ld_ch ld_adab ld_gn ld_rg ld_sgu ld_wsn ld_rows ld_router
            acc_zeroed zero_ready csilu tp_ready tp_evac mod_ready mod_evac sumsq sumsq_v rs_in rstd_ready
            mods_out mods_back mod_scaled xn_done xn_ready xn_free prj_ready prj_evac conv_step conv_done softp softp_exp
            gates_done expd lru_den lru_sqrt lru_u lru_h ya_sq gms_eps gms_sqrt ya_done msk gv_sq v_rs v_sqrt v_done
            yb_step yb_sqrt out_small_ready out_small wout_ready x2_done x2_sq rs2_in rs2 sc_done route_step routed
            logit_done mask_done tok_written sh_ready sh_act sh_hid sh_down_ready sh_evac final_gn gf_back
            xg_zero sel_built sel_ready idx_ready gate_ready xt_ready xt0_evac xt1_evac gu_done sg_evac up_evac hid_ready
            ht_ready ht_evac y_ready y0_evac y1_evac pool_go pad_set pos_shifted flags
            fin_step pre_done fin_sq fin_rs out_done gn_ffn gn_fin hc_done mix_free vq""".split()
        s = {n: sem(n) for n in names}
        ld_piece = [sem(f"ld_piece{i}") for i in range(SLOTS)]
        ld_gu = [sem(f"ld_gu{i}") for i in range(SLOTS)]
        ld_dn = [sem(f"ld_dn{i}") for i in range(SLOTS)]
        ld_shared_gu, ld_shared_dn = sem("ld_shared_gu"), sem("ld_shared_dn")
        gathered = [sem("gathered0"), sem("gathered1")]
        gathered2 = [sem("gathered2_0"), sem("gathered2_1")]
        scattered = [sem("scattered0"), sem("scattered1")]
        mods_out = [sem(f"mods_out{i}") for i in range(3)]
        mods_back = [sem(f"mods_back{i}") for i in range(3)]
        g_back = sem("g_back")
        acc_back = [sem(f"acc_back{t}") for t in range(3)]
        dve_link, act_link = sem("dve_link"), sem("act_link")

        ada_p = io["ada_w"][0].rearrange("(p k) (j n) -> j p k n", k=KT, n=512)
        win_p = io["w_in"][0].rearrange("(p k) (j n) -> j p k n", k=KT, n=512)
        wout_p = io["w_out"][0].rearrange("(k p) (j n) -> j p k n", p=P, n=512)
        eg = io["exp_w_gate"][0].rearrange("e (p k) f -> e p k f", k=KT)
        eu = io["exp_w_up"][0].rearrange("e (p k) f -> e p k f", k=KT)
        ed = io["exp_w_down"][0].rearrange("e (p j) n -> e p (j n)", j=2)

        PIECES = ([("ada", j) for j in range(4)] + [("in", 0), ("ada", 4), ("ada", 5), ("in", 1), ("ada", 6), ("ada", 7),
                  ("in", 3), ("ada", 8), ("ada", 9), ("in", 2), ("ada", 10), ("ada", 11), ("out", 0), ("out", 1)])
        NP = len(PIECES)
        piece_no = {pc: n for n, pc in enumerate(PIECES)}
        SH_NO = NP
        E_NO = NP + 1
        SH_SLOT = SH_NO % SLOTS

        def used(n):
            if n == SH_NO:
                return s["sh_ready"], 3
            kind, j = PIECES[n]
            if kind == "ada":
                return s["mod_ready"], j + 1
            if kind == "in":
                return s["prj_ready"], prj_no[[("xa", CT - 1), ("ga", CT - 1), ("u", 2), ("v", 2)][j]] + 1
            return s["wout_ready"], 6

        def gslot(u):
            return (E_NO + u) % SLOTS

        def dslot(u):
            return (1 + u) % SLOTS

        TP = {}
        for n in (["c", "ch", "w0", "w1", "ws"] + [f"x{t}{h}" for t in range(3) for h in range(2)]
                  + [f"g{c}" for c in range(CT)] + ["s0", "s1", "s2", "hc"] + ["y0", "y1", "y2"]
                  + [f"z{t}{h}" for t in range(3) for h in range(2)] + ["logit", "pos"] + ["h0", "h1", "h2"]):
            TP[n] = len(TP)

        def tp_bank(n):
            return bank[2 + TP[n] % 2]

        PRJ = ([("xa", c) for c in range(CT)] + [("ga", c) for c in range(CT)] + [("r", c) for c in range(CT)]
               + [("i", c) for c in range(CT)] + [("v", t) for t in range(3)] + [("u", t) for t in range(3)])
        prj_no = {n: i for i, n in enumerate(PRJ)}

        def prj_bank(n):
            return bank[4 + prj_no[n] % 4]
        WO_BANK = [4, 5, 6, 7, 0, 1]

        rstd = small[:, 0:3]
        ssq = small[:, 3:6]
        vss = small[:, 6:9]
        vrs = small[:, 9:12]
        s8 = small[:, 12:16]
        lam = chT[:, :, 39]
        sp = [small[:, 16 + 4 * n:20 + 4 * n] for n in range(8)]
        fss = small[:, 52:55]
        skipped = small[0:1, 16:16 + 2 * U]
        frs = small[:, 55:58]

        block = ctx.enter_context(nc.Block())

        @block.sync
        def _(sync):
            for n, (kind, j) in enumerate(PIECES):
                if n >= SLOTS:
                    sync.wait_ge(*used(n - SLOTS))
                src = {"ada": ada_p, "in": win_p, "out": wout_p}[kind][j]
                sync.dma_start(gu[n % SLOTS][:, :, :], src).then_inc(ld_piece[n % SLOTS], 16)
            sync.wait_ge(*used(SH_NO - SLOTS))
            for c, name in enumerate(("shared_w_gate", "shared_w_up")):
                sync.dma_start(gu[SH_SLOT][:, :, c * FE:(c + 1) * FE],
                               io[name][0].rearrange("(p k) f -> p k f", k=KT)).then_inc(ld_shared_gu, 16)

            def load_gu(r, i, u):
                g = r * NE + i * U + u
                if isinstance(g, int) and g < SLOTS:
                    sync.wait_ge(*used(E_NO + g - SLOTS))
                else:
                    sync.wait_ge(s["gu_done"], g - (SLOTS - 1))
                e = i * U + u
                sync.dma_start(gu[gslot(u)][:, :, 0:FE], eg[e]).then_inc(ld_gu[gslot(u)], 16)
                sync.dma_start(gu[gslot(u)][:, :, FE:2 * FE], eu[e]).then_inc(ld_gu[gslot(u)], 16)

            def load_dn(r, i, u):
                g = r * NE + i * U + u
                if isinstance(g, int) and g == SLOTS - 1:
                    sync.wait_ge(s["sh_down_ready"], 6)
                elif not (isinstance(g, int) and g < SLOTS):
                    sync.wait_ge(s["y_ready"], g - (SLOTS - 1))
                sync.dma_start(dn[:, dslot(u), :], ed[i * U + u]).then_inc(ld_dn[dslot(u)], 16)

            def back(i, u):
                return (i, u - 1) if u else (i - 1, U - 1)

            for u in range(3):
                load_gu(0, 0, u)
            sync.wait_ge(s["ya_done"], 4 * CT)
            sync.wait_ge(s["mix_free"], 1)
            sync.dma_start(dn[:, 0, :], io["shared_w_down"][0].rearrange("(p j) n -> p (j n)", j=2)).then_inc(ld_shared_dn, 16)
            for u in range(2):
                load_dn(0, 0, u)
            load_gu(0, 0, 3)
            load_dn(0, 0, 2)
            for u in range(4, U):
                load_gu(0, 0, u)
                load_dn(0, 0, u - 1)
            with sync.Fori(1, NE // U) as i:
                for u in range(U):
                    load_gu(0, i, u)
                    load_dn(0, *back(i, u))
            load_dn(0, NE // U - 1, U - 1)
            sync.wait_ge(s["flags"], 1)
            most = sync.value_load(cnt_i[0:1, NE:NE + 1], min_val=0, max_val=T)
            for r in range(1, ROUNDS):
                with sync.If(most > r * ROUND):
                    for u in range(U):
                        load_gu(r, 0, u)
                        if u:
                            load_dn(r, 0, u - 1)
                    with sync.Fori(1, NE // U) as i:
                        for u in range(U):
                            load_gu(r, i, u)
                            load_dn(r, *back(i, u))
                    load_dn(r, NE // U - 1, U - 1)
            sync.wait_ge(s["routed"], 1)
            sync.wait_ge(s["pre_done"], 3)
            for t, (t0, n) in enumerate(TILES):
                for b, dst in ((0, xn), (1, sh)):
                    sync.dma_start(dst[0:n, t, :], acc_rows[b][2 * t0:2 * (t0 + n), :].rearrange("(p h) n -> p (h n)", h=2)).then_inc(acc_back[t], 16)
            for t, (t0, n) in enumerate(TILES):
                sync.wait_ge(s["out_done"], t + 1)
                dst = io["y_prompt"][0, t0:t0 + n, :] if t < 2 else io["y_sample"].rearrange("b t n -> (b t) n")
                sync.dma_start(dst, xn[0:n, t, :]).then_inc(s["fin_step"], 16)
            sync.wait_ge(s["fin_step"], 48)
            sync.wait_ge(s["out_small"], 64)
            sync.wait_ge(s["v_out"], 16)

        @block.gpsimd
        def _(pool):
            pool.memset(ident[:, :], 0.0).then_inc(s["consts"], 1)
            pool.memset(ones[:, :], 1.0).then_inc(s["consts"], 1)
            pool.memset(upper[:, :], 1.0).then_inc(s["consts"], 1)
            pool.wait_ge(s["consts"], 3)
            pool.affine_select(out=ident[:, :], in_=ident[:, :], compare_op=ALU.not_equal, fill=1.0, base=0,
                               pattern=[[-1, P]], channel_multiplier=1).then_inc(s["consts"], 1)
            pool.affine_select(out=upper[:, :], in_=upper[:, :], compare_op=ALU.is_gt, fill=0.0, base=0,
                               pattern=[[1, P]], channel_multiplier=-1).then_inc(s["consts"], 1)
            pool.iota(iota_s[:, :], allow_small_or_imprecise_dtypes=True, pattern=[[64, 2], [0, 2], [1, 64]], base=0, channel_multiplier=0).then_inc(s["consts"], 1)
            pool.iota(tokc[:, :], allow_small_or_imprecise_dtypes=True, pattern=[[2 * P, 3]], base=-OOB, channel_multiplier=2).then_inc(s["consts"], 1)
            pool.wait_ge(s["zero_ready"], 1)
            for b in range(2):
                pool.dma_start(acc_rows[b].rearrange("(p a) n -> p (a n)", p=P), dnf[:, 0:2560]).then_inc(s["acc_zeroed"], 16)
            pool.wait_ge(s["ld_sgu"], 16)
            pool.affine_select(out=wnat, in_=wnat, compare_op=ALU.is_ge, fill=0.0, base=0,
                               pattern=[[0, 8], [-1, P]], channel_multiplier=1).then_inc(s["msk"], 1)
            pool.wait_ge(s["ld_wsn"], 16 * NB)
            pool.affine_select(out=wsn[0:64, :, :], in_=wsn[0:64, :, :], compare_op=ALU.is_ge, fill=0.0, base=0,
                               pattern=[[0, 8], [-1, 64]], channel_multiplier=1).then_inc(s["msk"], 1)

            def mods_to_rows(part_no, j0, j1):
                pool.wait_ge(s["mod_evac"], j1)
                dst = mod_rows.rearrange("b (j g n) -> b j g n", j=12, g=4)
                for g in range(4):
                    pool.dma_start(dst[:, j0:j1, g, :], mods[32 * g:32 * g + NSEQ, j0:j1, :]).then_inc(mods_out[part_no], 16)
                pool.wait_ge(mods_out[part_no], 64)

            def spread(dst, chunk, sm):
                src = mod_rows[:, chunk * D:(chunk + 1) * D]
                pool.dma_start(dst[:, 0, :], src[0:1, :].to_broadcast([P, D])).then_inc(sm, 16)
                pool.dma_start(dst[0:64, 1, :], src[1:NSEQ, :].rearrange("b (o n) -> b o n", o=1)
                               .to_broadcast([NB, NT, D])).then_inc(sm, 16)

            mods_to_rows(0, 0, 4)
            spread(mb[:, 0], 1, mods_back[0])
            spread(mb[:, 1], 0, mods_back[0])
            mods_to_rows(1, 4, 6)
            spread(gmod, 2, mods_back[1])
            pool.wait_ge(s["xn_done"], 3)
            mods_to_rows(2, 6, 12)
            spread(mb[:, 0], 4, mods_back[2])
            spread(mb[:, 1], 3, mods_back[2])
            pool.wait_ge(s["v_done"], 3)
            pool.dma_start(io["v_sample"].rearrange("o b t n -> (o b t) n"), vv[0:64, 2, :]).then_inc(s["v_out"], 16)
            pool.wait_ge(s["hc_done"], 1)
            pool.dma_start(io["h_prompt"].rearrange("o b n -> (o b) n"), hrow[0:1, :]).then_inc(s["out_small"], 16)
            pool.dma_start(io["h_sample"].rearrange("o b n -> (o b) n"), hrow[1:9, :]).then_inc(s["out_small"], 16)
            pool.dma_start(io["conv_prompt"].rearrange("o b j n -> (o b j) n"), hrow[9:12, :]).then_inc(s["out_small"], 16)
            pool.dma_start(io["conv_sample"].rearrange("o b j n -> (o b j) n"), hrow[12:36, :]).then_inc(s["out_small"], 16)
            pool.wait_ge(s["x2_done"], 3)
            spread(gmod, 5, g_back)
            pool.memset(et[:, 0:2048], 0.0).then_inc(s["xg_zero"], 1)
            for t, (t0, n) in enumerate(TILES):
                pool.wait_ge(s["xn_ready"], t + 1)
                pool.dma_start(xn_rows[t0:t0 + n, :], xn[0:n, t, :]).then_inc(s["tok_written"], 16)
            pool.wait_ge(s["tok_written"], 48)
            pool.wait_ge(s["xg_zero"], 1)
            pool.wait_ge(s["acc_zeroed"], 32)

            def is_full(r, i, u):
                return pool.value_load(cnt_i[0:1, bass.ds(i * U + u, 1)], min_val=0, max_val=T) > (r * ROUND + 64)

            def gather(r, i, u):
                e = r * NE + i * U + u
                full = is_full(r, i, u)
                pool.wait_ge(s["idx_ready"], e + 1)
                if not (isinstance(e, int) and e < 2):
                    pool.wait_ge(s["xt_ready"], e - 1)
                pool.sem_inc(s["pool_go"], 1)
                pool.indirect_dma_start(xg[:, u % 2, 0, :], None, xn_half,
                                        bass.IndirectOffsetOnAxis(ap=idx[:, u, 0:1], axis=0),
                                        bounds_check=2 * T - 1, oob_is_err=False).then_inc(gathered[u % 2], 16)
                with pool.If(full):
                    pool.indirect_dma_start(xg[:, u % 2, 1, :], None, xn_half,
                                            bass.IndirectOffsetOnAxis(ap=idx[:, u, 1:2], axis=0),
                                            bounds_check=2 * T - 1, oob_is_err=False).then_inc(gathered2[u % 2], 16)
                with pool.Else():
                    pool.dma_start(skipped[:, u:u + 1], halfc[0:1, :]).then_inc(gathered2[u % 2], 16)

            def scatter(r, i, u):
                e = r * NE + i * U + u
                full = is_full(r, i, u)
                pool.wait_ge(s["y0_evac"], e + 1)
                if not (isinstance(e, int) and e == 0):
                    pool.wait_ge(scattered[0], 16 * e)
                pool.sem_inc(s["pool_go"], 1)
                pool.indirect_dma_start(acc_rows[0], bass.IndirectOffsetOnAxis(ap=idx[:, u, 0:1], axis=0),
                                        yo[:, u % 2, 0, :], None, bounds_check=2 * T - 1, oob_is_err=False,
                                        compute_op=ALU.add).then_inc(scattered[0], 16)
                pool.wait_ge(s["y1_evac"], e + 1)
                if not (isinstance(e, int) and e == 0):
                    pool.wait_ge(scattered[1], 16 * e)
                pool.sem_inc(s["pool_go"], 1)
                with pool.If(full):
                    pool.indirect_dma_start(acc_rows[1], bass.IndirectOffsetOnAxis(ap=idx[:, u, 1:2], axis=0),
                                            yo[:, u % 2, 1, :], None, bounds_check=2 * T - 1, oob_is_err=False,
                                            compute_op=ALU.add).then_inc(scattered[1], 16)
                with pool.Else():
                    pool.dma_start(skipped[:, U + u:U + u + 1], halfc[0:1, :]).then_inc(scattered[1], 16)

            def body(r, i, first=False, last=False):
                for u in range(U):
                    if not (last and u >= U - 2):
                        gather(r, i + (u + 2) // U, (u + 2) % U)
                    if not (first and u == 0):
                        scatter(r, i if u else i - 1, (u - 1) % U)

            def rounds(r):
                gather(r, 0, 0)
                gather(r, 0, 1)
                body(r, 0, first=True)
                with pool.Fori(1, NE // U - 1) as i:
                    body(r, i)
                body(r, NE // U - 1, last=True)
                scatter(r, NE // U - 1, U - 1)
                for b in range(2):
                    pool.wait_ge(scattered[b], 16 * NE * (r + 1))

            pool.wait_ge(s["flags"], 1)
            rounds(0)
            most = pool.value_load(cnt_i[0:1, NE:NE + 1], min_val=0, max_val=T)
            for r in range(1, ROUNDS):
                with pool.If(most > r * ROUND):
                    rounds(r)
            pool.sem_inc(s["routed"], 1)

        @block.scalar
        def _(act):
            nl = [0]

            def link(ins):
                nl[0] += 1
                ins.then_inc(act_link, 1)
                act.wait_ge(act_link, nl[0])

            act.wait_ge(s["crow_zero"], 1)
            act.dma_start(crow[0:1, :], io["c_prompt"]).then_inc(s["ld_c"], 16)
            act.dma_start(crow[1:NSEQ, :], io["c_sample"]).then_inc(s["ld_c"], 16)
            act.dma_start(x[:, 0:2, :], io["x_prompt"][0].rearrange("(t p) n -> p t n", p=P)).then_inc(s["ld_x"], 16)
            act.dma_start(x[0:64, 2, :], io["x_sample"].rearrange("b t n -> (b t) n")).then_inc(s["ld_x"], 16)
            rows = [(0, io["state_conv"][0].rearrange("b j n -> (b j) n")), (24, io["state_lru_h"][0]), (32, io["conv_w"][0]),
                    (36, io["conv_b"]), (37, io["gate_r_b"]), (38, io["gate_i_b"]), (39, io["lru_lambda"]),
                    (40, io["out_norm_g"][:, 0:W])]
            for r0, src in rows:
                act.dma_start(chrow[r0:r0 + src.shape[0], :], src).then_inc(s["ld_ch"], 16)
            act.dma_start(wnat, io["sgu_w"][0].rearrange("g p q -> p g q")).then_inc(s["ld_sgu"], 16)
            bsrc = io["ada_b"].rearrange("o (j g n) -> o j g n", j=12, g=4)
            for g in range(4):
                act.dma_start(adab[32 * g:32 * g + 32], bsrc[:, :, g, :].to_broadcast([32, 12, P])).then_inc(s["ld_adab"], 16)
            act.dma_start(gn[:, :], io["norm_mix_g"].to_broadcast([P, D])).then_inc(s["ld_gn"], 16)
            act.wait_ge(s["blk_zero"], 3)
            for wt, name in ((wr, "gate_r_w"), (wi, "gate_i_w")):
                for h in range(2):
                    act.dma_start(wt[64 * h:64 * h + 64, :, 64 * h:64 * h + 64],
                                  io[name][0].rearrange("(c h) i j -> h i c j", h=2)[h]).then_inc(s["ld_rg"], 16)
            for b in range(NB):
                act.dma_start(wsn[8 * b:8 * b + 8, :, 8 * b:8 * b + 8],
                              io["sgu_w"][0, :, 0:NT, 0:NT].rearrange("g p q -> p g q")).then_inc(s["ld_wsn"], 16)
            act.dma_start(vg_row, io["sgu_norm_g"].to_broadcast([P, W])).then_inc(s["ld_rows"], 16)
            act.dma_start(og_row, io["out_norm_g"][:, W:2 * W].to_broadcast([P, W])).then_inc(s["ld_rows"], 16)
            act.dma_start(bsT, io["sgu_b"][0].rearrange("g p -> p g")).then_inc(s["ld_rows"], 16)
            for b in range(NB):
                act.dma_start(bsS[8 * b:8 * b + 8, :], io["sgu_b"][0, :, 0:NT].rearrange("g p -> p g")).then_inc(s["ld_rows"], 16)
            act.dma_start(wrt[:, :, :], io["router_w"][0].rearrange("(p k) e -> p k e", k=KT)).then_inc(s["ld_router"], 16)
            act.dma_start(rbias[:, :], io["router_bias"].to_broadcast([P, NE])).then_inc(s["ld_router"], 16)

            act.wait_ge(s["ld_c"], 32)
            act.activation(crow, crow, ACT.Silu).then_inc(s["csilu"], 1)
            act.wait_ge(s["ld_x"], 32)
            act.wait_ge(s["sumsq_v"], 2)
            for t, (t0, n) in enumerate(TILES):
                act.activation(xn[0:n, t, :], x[0:n, t, :], ACT.Square, accum_out=ssq[0:n, t:t + 1]).then_inc(s["sumsq"], 1)
            act.wait_ge(s["rs_in"], 4)
            act.activation(rstd, rstd, ACT.Sqrt).then_inc(s["rstd_ready"], 1)
            act.wait_ge(s["softp"], 2)
            act.activation(sp[1], sp[1], ACT.Exp, scale=-1.0).then_inc(s["softp_exp"], 1)

            act.wait_ge(s["mod_scaled"], 2)
            act.dma_start(gn[:, :], io["norm_ffn_g"].to_broadcast([P, D])).then_inc(s["gn_ffn"], 16)

            def prj(kind, n):
                act.wait_ge(s["prj_ready"], prj_no[(kind, n)] + 1)
                return prj_bank((kind, n))

            act.wait_ge(s["conv_step"], 2)
            for c in range(CT):
                b = prj("xa", c)
                link(act.activation(xap[:, c, CW - 1:SEG], b[:, 0:NPR], ACT.Copy))
                act.activation(xap[:, c, SEG:].rearrange("p (b j) -> p b j", b=NB)[:, :, CW - 1:],
                               b[:, NPR:T].rearrange("p (b j) -> p b j", b=NB), ACT.Copy).then_inc(s["prj_evac"], 1)
            for c in range(CT):
                act.activation(ga[:, c, :], prj("ga", c)[:, 0:T], ACT.Gelu_apprx_tanh).then_inc(s["prj_evac"], 1)
            for c in range(CT):
                act.activation(rr[:, c, :], prj("r", c)[:, 0:T], ACT.Sigmoid, bias=chT[:, c, 37:38]).then_inc(s["prj_evac"], 1)
            for c in range(CT):
                act.activation(ii[:, c, :], prj("i", c)[:, 0:T], ACT.Sigmoid, bias=chT[:, c, 38:39]).then_inc(s["prj_evac"], 1)
            act.wait_ge(s["prj_evac"], prj_no[("i", CT - 1)] + 1)
            act.wait_ge(s["softp"], 15)
            for c in range(CT):
                act.activation(aa[:, c, :], rr[:, c, :], ACT.Exp, scale=s8[:, c:c + 1]).then_inc(s["expd"], 1)
            act.wait_ge(s["expd"], CT)
            for c in range(CT):
                act.activation(rr[:, c, :], rr[:, c, :], ACT.Tanh, scale=s8[:, c:c + 1]).then_inc(s["expd"], 1)
            act.wait_ge(s["lru_den"], 3)
            act.activation(rr, rr, ACT.Sqrt).then_inc(s["lru_sqrt"], 1)
            act.wait_ge(s["xn_free"], 1)
            for t, (t0, n) in enumerate(TILES):
                act.activation(vv[0:n, t, :], prj("v", t)[0:n, :], ACT.Gelu_apprx_tanh).then_inc(s["prj_evac"], 1)
            for t, (t0, n) in enumerate(TILES):
                act.wait_ge(s["prj_evac"], prj_no[("v", t)] + 1)
                act.activation(us[0:n, t, :], vv[0:n, t, :], ACT.Square, accum_out=vss[0:n, t:t + 1]).then_inc(s["gv_sq"], 1)
            act.wait_ge(s["v_rs"], 4)
            act.activation(vrs, vrs, ACT.Sqrt).then_inc(s["v_sqrt"], 1)
            act.wait_ge(s["gms_eps"], 5)
            act.activation(dd, dd, ACT.Sqrt).then_inc(s["gms_sqrt"], 1)
            for t, (t0, n) in enumerate(TILES):
                if t == 0:
                    act.wait_ge(s["gv_sq"], 3)
                act.activation(us[0:n, t, :], prj("u", t)[0:n, :], ACT.Gelu_apprx_tanh).then_inc(s["prj_evac"], 1)
            for t, (t0, n) in enumerate(TILES):
                act.wait_ge(s["yb_step"], 7 * t + 6)
                act.activation(small[0:n, 16:24], small[0:n, 16:24], ACT.Sqrt).then_inc(s["yb_sqrt"], 1)
            for t, (t0, n) in enumerate(TILES):
                act.wait_ge(s["x2_done"], t + 1)
                act.activation(sqy[0:n, :], x[0:n, t, :], ACT.Square, accum_out=ssq[0:n, t:t + 1]).then_inc(s["x2_sq"], 1)
                act.wait_ge(s["rs2_in"], 2 * t + 2)
                act.activation(rstd[0:n, t:t + 1], rstd[0:n, t:t + 1], ACT.Sqrt).then_inc(s["rs2"], 1)
            act.wait_ge(s["tp_ready"], TP["logit"] + 1)
            act.wait_ge(s["pad_set"], 2)
            for t, (t0, n) in enumerate(TILES):
                act.activation(score[0:n, t, :], tp_bank("logit")[0:n, t * NE:(t + 1) * NE], ACT.Sigmoid).then_inc(s["sc_done"], 1)
            for t, (t0, n) in enumerate(TILES):
                act.wait_ge(s["sh_ready"], t + 1)
                if t:
                    act.wait_ge(s["sh_hid"], t)
                act.activation(sgs[0:n, :], bank[4 + t][0:n, 0:FE], ACT.Silu).then_inc(s["sh_act"], 1)
            act.wait_ge(s["out_small"], 64)
            for t, (t0, n) in enumerate(TILES):
                for c in range(2):
                    act.wait_ge(s["sh_down_ready"], 2 * t + c + 1)
                    act.activation(sh[0:n, t, c * HALF:(c + 1) * HALF], bank[(2 * t + c) % 2][0:n, :], ACT.Copy).then_inc(s["sh_evac"], 1)

            def xt1(r, i, u):
                act.wait_ge(s["xt_ready"], r * NE + i * U + u + 1)
                act.activation(xt[:, 1].rearrange("p k h n -> p (k h n)"), bank[3][:, :], ACT.Copy).then_inc(s["xt1_evac"], 1)

            def gates(r, i, u):
                e = r * NE + i * U + u
                act.wait_ge(s["gu_done"], e + 1)
                if not (isinstance(e, int) and e == 0):
                    act.wait_ge(s["hid_ready"], e)
                act.activation(sg[0:64, :], bank[u % 2][0:64, :], ACT.Silu).then_inc(s["sg_evac"], 1)
                act.activation(up[0:64, :], bank[u % 2][64:P, :], ACT.Copy).then_inc(s["up_evac"], 1)

            def y1(r, i, u):
                e = r * NE + i * U + u
                act.wait_ge(s["y_ready"], e + 1)
                act.wait_ge(s["idx_ready"], e + 1)
                if not (isinstance(e, int) and e < 2):
                    act.wait_ge(scattered[1], 16 * e - 16)
                act.activation(yo[:, u % 2, 1, :], bank[6][:, :], ACT.Copy, scale=pick_out[:, u, 1, 1:2]).then_inc(s["y1_evac"], 1)

            def body(r, i, first=False, last=False):
                for u in range(U):
                    gates(r, i, u)
                    if not (last and u == U - 1):
                        xt1(r, i + (u + 1) // U, (u + 1) % U)
                    if not (first and u == 0):
                        y1(r, i if u else i - 1, (u - 1) % U)

            def rounds(r):
                xt1(r, 0, 0)
                body(r, 0, first=True)
                with act.Fori(1, NE // U - 1) as i:
                    body(r, i)
                body(r, NE // U - 1, last=True)
                y1(r, NE // U - 1, U - 1)

            rounds(0)
            most = act.value_load(cnt_i[0:1, NE:NE + 1], min_val=0, max_val=T)
            for r in range(1, ROUNDS):
                with act.If(most > r * ROUND):
                    rounds(r)
            act.dma_start(gn[:, :], io["final_norm_g"].rearrange("(o n) -> o n", o=1).to_broadcast([P, D])).then_inc(s["gn_fin"], 16)
            for t, (t0, n) in enumerate(TILES):
                act.wait_ge(s["fin_sq"], 3 * t + 3)
                act.activation(sqy[0:n, :], xn[0:n, t, :], ACT.Square, accum_out=fss[0:n, t:t + 1]).then_inc(s["fin_rs"], 1)
                act.wait_ge(s["rs_in"], 4 + 2 * t + 2)
                act.activation(frs[0:n, t:t + 1], frs[0:n, t:t + 1], ACT.Sqrt).then_inc(s["fin_rs"], 1)

        @block.tensor
        def _(pe):
            def tp_wait(n):
                if TP[n] >= 2:
                    pe.wait_ge(s["tp_evac"], TP[n] - 1)
                return tp_bank(n)

            def piece(kind, j):
                n = piece_no[(kind, j)]
                pe.wait_ge(ld_piece[n % SLOTS], 16 * (n // SLOTS + 1))
                return gu[n % SLOTS]

            def ada(j):
                w = piece("ada", j)
                if j >= 2:
                    pe.wait_ge(s["mod_evac"], j - 1)
                for k in range(KT):
                    for g in range(4):
                        mm = pe.matmul(bank[j % 2][32 * g:32 * g + 32, 0:P], cT[:, k, :], w[:, k, g * P:(g + 1) * P],
                                       start=(k == 0), stop=(k == KT - 1))
                mm.then_inc(s["mod_ready"], 1)

            def prj_wait(kind, n):
                no = prj_no[(kind, n)]
                if no >= 4:
                    pe.wait_ge(s["prj_evac"], no - 3)
                return prj_bank((kind, n))

            def channels(kind, j):
                w = piece("in", j)
                for c in range(CT):
                    b = prj_wait(kind, c)
                    for k in range(KT):
                        mm = pe.matmul(b[:, 0:T], w[:, k, c * P:(c + 1) * P], xT[:, k, :], start=(k == 0), stop=(k == KT - 1))
                    mm.then_inc(s["prj_ready"], 1)

            def tokens(kind, j):
                w = piece("in", j)
                for t, (t0, n) in enumerate(TILES):
                    b = prj_wait(kind, t)
                    for k in range(KT):
                        mm = pe.matmul(b[0:n, :], xT[:, k, t0:t0 + n], w[:, k, :], start=(k == 0), stop=(k == KT - 1))
                    mm.then_inc(s["prj_ready"], 1)

            pe.wait_ge(s["consts"], 7)
            pe.wait_ge(s["csilu"], 1)
            pe.wait_ge(s["consts_v"], 5)
            b = tp_wait("c")
            for k in range(KT):
                mm = pe.transpose(b[:, 32 * k:32 * k + 32], crow[:, k::KT], ident[0:32, 0:32])
            mm.then_inc(s["tp_ready"], 1)
            pe.wait_ge(s["ld_ch"], 16 * 8)
            b = tp_wait("ch")
            for c in range(CT):
                mm = pe.transpose(b[:, 41 * c:41 * c + 41], chrow[0:41, c * P:(c + 1) * P], ident[0:41, 0:41])
            mm.then_inc(s["tp_ready"], 1)
            pe.wait_ge(s["tp_evac"], 1)
            for j in range(4):
                ada(j)
            pe.wait_ge(s["msk"], 2)
            for h in range(2):
                b = tp_wait(f"w{h}")
                for g in range(4):
                    mm = pe.transpose(b[:, g * P:(g + 1) * P], wnat[:, 4 * h + g, :], ident[:, :])
                mm.then_inc(s["tp_ready"], 1)
            b = tp_wait("ws")
            for g in range(8):
                mm = pe.transpose(b[0:64, g * 64:(g + 1) * 64], wsn[0:64, g, :], ident[0:64, 0:64])
            mm.then_inc(s["tp_ready"], 1)

            def turn(name, done, t):
                t0, n = TILES[t]
                pe.wait_ge(s[done], t + 1)
                for h in range(2):
                    b = tp_wait(f"{name}{t}{h}")
                    for k in range(4):
                        mm = pe.transpose(b[:, k * P:k * P + n], xn[0:n, t, (4 * h + k) * P:(4 * h + k + 1) * P], ident[0:n, 0:n])
                    mm.then_inc(s["tp_ready"], 1)

            for t in range(3):
                turn("x", "xn_done", t)
            pe.wait_ge(s["tp_evac"], TP["x21"] + 1)
            channels("xa", 0)
            ada(4)
            ada(5)
            channels("ga", 1)
            pe.wait_ge(s["ld_rg"], 64)
            pe.wait_ge(s["conv_done"], 1)
            for kind, wt in (("r", wr), ("i", wi)):
                for c in range(CT):
                    pe.matmul(prj_wait(kind, c)[:, 0:T], wt[:, c, :], xc[:, c, :], start=True, stop=True).then_inc(s["prj_ready"], 1)
            ada(6)
            ada(7)
            tokens("v", 3)
            ada(8)
            ada(9)
            pe.wait_ge(s["ya_sq"], 2)
            for c in range(CT):
                pe.matmul(tp_wait(f"g{c}")[:, 0:T], blk[:, :], dd[:, c, :], start=True, stop=True).then_inc(s["tp_ready"], 1)
            tokens("u", 2)
            ada(10)
            ada(11)
            pe.wait_ge(s["v_done"], 3)
            for t, (t0, n) in enumerate(TILES):
                b = tp_wait(f"s{t}")
                for g in range(8):
                    w = wT[:, g, :] if t < 2 else wsT[0:64, g, :]
                    mm = pe.matmul(b[0:n, g * 64:(g + 1) * 64], w, vv[0:n, t, g * 64:(g + 1) * 64], start=True, stop=True)
                mm.then_inc(s["tp_ready"], 1)
            w = [piece("out", 0), piece("out", 1)]
            pe.wait_ge(s["prj_evac"], len(PRJ))
            pe.wait_ge(s["mod_evac"], 12)
            pe.wait_ge(s["ya_done"], 4 * CT)
            for q in range(6):
                t0, n = TILES[q // 2]
                for k in range(4):
                    pe.matmul(bank[WO_BANK[q]][0:n, :], xT[:, k, t0:t0 + n], w[q % 2][:, k, :], start=(k == 0), stop=False)
            pe.wait_ge(s["lru_h"], 2)
            b = tp_wait("hc")
            for c in range(CT):
                mm = pe.transpose(b[0:36, c * P:(c + 1) * P], hc[:, c, :], ident[:, :])
            mm.then_inc(s["tp_ready"], 1)
            for t, (t0, n) in enumerate(TILES):
                pe.wait_ge(s["yb_step"], 7 * t + 7)
                b = tp_wait(f"y{t}")
                for k in range(4):
                    mm = pe.transpose(b[:, k * P:k * P + n], us[0:n, t, k * P:(k + 1) * P], ident[0:n, 0:n])
                mm.then_inc(s["tp_ready"], 1)
            for q in range(6):
                t0, n = TILES[q // 2]
                pe.wait_ge(s["tp_evac"], TP[f"y{q // 2}"] + 1)
                for k in range(4, KT):
                    mm = pe.matmul(bank[WO_BANK[q]][0:n, :], xT[:, k, t0:t0 + n], w[q % 2][:, k, :], start=False, stop=(k == KT - 1))
                mm.then_inc(s["wout_ready"], 1)
            for t in range(3):
                turn("z", "xn_ready", t)
            pe.wait_ge(s["tp_evac"], TP["z21"] + 1)
            pe.wait_ge(s["ld_router"], 32)
            b = tp_wait("logit")
            for t, (t0, n) in enumerate(TILES):
                for k in range(KT):
                    mm = pe.matmul(b[0:n, t * NE:(t + 1) * NE], xT[:, k, t0:t0 + n], wrt[:, k, :], start=(k == 0), stop=(k == KT - 1))
            mm.then_inc(s["tp_ready"], 1)
            pe.wait_ge(ld_shared_gu, 32)
            pe.wait_ge(s["x2_done"], 3)
            for t, (t0, n) in enumerate(TILES):
                for k in range(KT):
                    mm = pe.matmul(bank[4 + t][0:n, :], xT[:, k, t0:t0 + n], gu[SH_SLOT][:, k, :], start=(k == 0), stop=(k == KT - 1))
                mm.then_inc(s["sh_ready"], 1)
            pe.wait_ge(s["mask_done"], 1)
            b = tp_wait("pos")
            for t, (t0, n) in enumerate(TILES):
                for q in range(t + 1):
                    m = TILES[q][1]
                    mm = pe.matmul(b[0:n, t * NE:(t + 1) * NE], (upper if q == t else ones)[0:m, 0:n], mask[0:m, q, :],
                                   start=(q == 0), stop=(q == t))
            for q in range(3):
                m = TILES[q][1]
                mm = pe.matmul(b[:, 3 * NE:4 * NE], ones[0:m, :], mask[0:m, q, :], start=(q == 0), stop=(q == 2))
            mm.then_inc(s["tp_ready"], 1)
            for t, (t0, n) in enumerate(TILES):
                pe.wait_ge(s["sh_hid"], t + 1)
                b = tp_wait(f"h{t}")
                for j in range(2):
                    mm = pe.transpose(b[:, j * P:j * P + n], shid[0:n, j * P:(j + 1) * P], ident[0:n, 0:n])
                mm.then_inc(s["tp_ready"], 1)
                pe.wait_ge(s["tp_evac"], TP[f"h{t}"] + 1)
                if t == 0:
                    pe.wait_ge(ld_shared_dn, 16)
                for c in range(2):
                    if 2 * t + c >= 2:
                        pe.wait_ge(s["sh_evac"], 2 * t + c - 1)
                    for j in range(2):
                        mm = pe.matmul(bank[(2 * t + c) % 2][0:n, :], shT[:, j, 0:n],
                                       dn[:, 0, j * D + c * HALF:j * D + (c + 1) * HALF], start=(j == 0), stop=(j == 1))
                    mm.then_inc(s["sh_down_ready"], 1)

            def pick(r, i, u):
                e = r * NE + i * U + u
                pe.wait_ge(s["sel_built"], e + 1)
                if isinstance(e, int) and e == 0:
                    pe.wait_ge(s["sh_hid"], 3)
                else:
                    pe.wait_ge(s["gate_ready"], e)
                for b in range(2):
                    for t, (t0, n) in enumerate(TILES):
                        mm = pe.matmul(bank[7][:, 6 * b:6 * b + 6], sel[0:n, t, b * P:(b + 1) * P],
                                       tg[0:n, t, bass.ds(i * U + u, 1)].rearrange("p e c m -> p (e c m)"),
                                       start=(t == 0), stop=(t == 2))
                mm.then_inc(s["sel_ready"], 1)

            def turn_x(r, i, u, full):
                e = r * NE + i * U + u
                pe.wait_ge(gathered[u % 2], 8 * (e - u % 2) + 16)
                pe.wait_ge(gathered2[u % 2], 8 * (e - u % 2) + 16)
                if isinstance(e, int) and e == 0:
                    pe.wait_ge(s["sc_done"], 3)
                    pe.wait_ge(s["tp_evac"], len(TP))
                else:
                    pe.wait_ge(s["xt0_evac"], e)
                    pe.wait_ge(s["xt1_evac"], e)

                def half(b):
                    for k in range(4):
                        pe.transpose(bank[2 + b][:, k * P:(k + 1) * P], xg[:, u % 2, b, k * P:(k + 1) * P], ident[:, :])
                with pe.If(full):
                    half(1)
                for k in range(4):
                    mm = pe.transpose(bank[2][:, k * P:(k + 1) * P], xg[:, u % 2, 0, k * P:(k + 1) * P], ident[:, :])
                mm.then_inc(s["xt_ready"], 1)

            def gate_up(r, i, u, full):
                e = r * NE + i * U + u
                pe.wait_ge(ld_gu[gslot(u)], 8 * (e - u % SLOTS) + 32)
                pe.wait_ge(s["xt0_evac"], e + 1)
                pe.wait_ge(s["xt1_evac"], e + 1)
                if isinstance(e, int) and e < 2:
                    pe.wait_ge(s["sh_evac"], 6)
                else:
                    pe.wait_ge(s["up_evac"], e - 1)
                w = gu[gslot(u)]

                def blocks(b):
                    for k in range(KT):
                        for c in range(2):
                            mm = pe.matmul(bank[u % 2][64 * c:64 * c + 64, b * FE:(b + 1) * FE], xt[:, b, k % 4, k // 4, :],
                                           w[:, k, c * FE:(c + 1) * FE], start=(k == 0), stop=(k == KT - 1))
                    return mm
                with pe.If(full):
                    blocks(1)
                blocks(0).then_inc(s["gu_done"], 1)

            def turn_h(r, i, u, full):
                e = r * NE + i * U + u
                pe.wait_ge(s["hid_ready"], e + 1)
                if not (isinstance(e, int) and e == 0):
                    pe.wait_ge(s["ht_evac"], e)

                def half(b):
                    for j in range(2):
                        mm = pe.transpose(bank[4][:, (2 * b + j) * 64:(2 * b + j + 1) * 64], hid[0:64, b, j, :], ident[0:64, 0:64])
                    return mm
                with pe.If(full):
                    half(1)
                half(0).then_inc(s["ht_ready"], 1)

            def down(r, i, u, full):
                e = r * NE + i * U + u
                pe.wait_ge(ld_dn[dslot(u)], 4 * (e - u % SLOTS) + 16)
                pe.wait_ge(s["ht_evac"], e + 1)
                if not (isinstance(e, int) and e == 0):
                    pe.wait_ge(s["y0_evac"], e)
                    pe.wait_ge(s["y1_evac"], e)

                def blocks(b):
                    for j in range(2):
                        for c in range(2):
                            mm = pe.matmul(bank[5 + b][64 * c:64 * c + 64, :], hT[:, b, j, :],
                                           dn[:, dslot(u), j * D + c * HALF:j * D + (c + 1) * HALF], start=(j == 0), stop=(j == 1))
                    return mm
                with pe.If(full):
                    blocks(1)
                blocks(0).then_inc(s["y_ready"], 1)

            def is_full(r, i, u):
                return pe.value_load(cnt_i[0:1, bass.ds(i * U + u, 1)], min_val=0, max_val=T) > (r * ROUND + 64)

            def body(r, i, first=False, last=False):
                now = is_full(r, i, 0)
                before = None if first else is_full(r, i - 1, U - 1)
                for u in range(U):
                    gate_up(r, i, u, now)
                    if before is not None:
                        turn_h(r, i if u else i - 1, (u - 1) % U, before)
                    if not (last and u >= U - 2):
                        pick(r, i + (u + 2) // U, (u + 2) % U)
                    after = None
                    if not (last and u == U - 1):
                        after = is_full(r, i + (u + 1) // U, (u + 1) % U)
                        turn_x(r, i + (u + 1) // U, (u + 1) % U, after)
                    if before is not None:
                        down(r, i if u else i - 1, (u - 1) % U, before)
                    before, now = now, after
                return before

            def rounds(r):
                pick(r, 0, 0)
                pick(r, 0, 1)
                turn_x(r, 0, 0, is_full(r, 0, 0))
                body(r, 0, first=True)
                with pe.Fori(1, NE // U - 1) as i:
                    body(r, i)
                before = body(r, NE // U - 1, last=True)
                turn_h(r, NE // U - 1, U - 1, before)
                down(r, NE // U - 1, U - 1, before)

            pe.wait_ge(s["flags"], 1)
            rounds(0)
            most = pe.value_load(cnt_i[0:1, NE:NE + 1], min_val=0, max_val=T)
            for r in range(1, ROUNDS):
                with pe.If(most > r * ROUND):
                    rounds(r)

        @block.vector
        def _(dve):
            nl = [0]

            def link(ins):
                nl[0] += 1
                ins.then_inc(dve_link, 1)
                dve.wait_ge(dve_link, nl[0])

            def tp_get(n):
                dve.wait_ge(s["tp_ready"], TP[n] + 1)
                return tp_bank(n)

            dve.memset(crow, 0.0).then_inc(s["crow_zero"], 1)
            dve.memset(dnf[:, 0:2560], 0.0).then_inc(s["zero_ready"], 1)
            dve.memset(wr, 0.0).then_inc(s["blk_zero"], 1)
            dve.memset(wi, 0.0).then_inc(s["blk_zero"], 1)
            dve.memset(wsn[0:64], 0.0).then_inc(s["blk_zero"], 1)
            dve.memset(xap[:, :, 0:CW - 1], 0.0).then_inc(s["conv_step"], 1)
            dve.memset(ssq, 1.0).then_inc(s["sumsq_v"], 1)
            dve.memset(vss, 1.0).then_inc(s["sumsq_v"], 1)
            dve.memset(halfc[0:64, :], float(OOB)).then_inc(s["consts_v"], 1)
            dve.memset(halfc[64:P, :], float(OOB + 1)).then_inc(s["consts_v"], 1)
            dve.memset(blk[:, :], 0.0).then_inc(s["consts_v"], 1)
            dve.wait_ge(s["consts_v"], 3)
            dve.memset(blk[0:64, 0:64], 1.0 / 64).then_inc(s["consts_v"], 1)
            dve.memset(blk[64:P, 64:P], 1.0 / 64).then_inc(s["consts_v"], 1)
            dve.wait_ge(s["consts"], 7)
            dve.tensor_copy(cT[:, :, :], tp_get("c")[:, 0:256].rearrange("p (k c) -> p k c", k=KT)).then_inc(s["tp_evac"], 1)
            dve.tensor_copy(chT[:, :, :], tp_get("ch")[:, 0:41 * CT].rearrange("p (c r) -> p c r", c=CT)).then_inc(s["tp_evac"], 1)
            dve.wait_ge(s["sumsq_v"], 2)
            dve.wait_ge(s["sumsq"], 3)
            for t, (t0, n) in enumerate(TILES):
                dve.tensor_scalar(rstd[0:n, t:t + 1], ssq[0:n, t:t + 1], 1.0 / D, EPS, ALU.mult, ALU.add).then_inc(s["rs_in"], 1)
            dve.wait_ge(s["rs_in"], 3)
            dve.memset(rstd[64:P, 2:3], 1.0).then_inc(dve_link, 1)
            nl[0] += 1
            dve.wait_ge(dve_link, nl[0])
            dve.reciprocal(rstd, rstd).then_inc(s["rs_in"], 1)
            sf = [0]

            def soft(ins):
                sf[0] += 1
                ins.then_inc(s["softp"], 1)
                dve.wait_ge(s["softp"], sf[0])
            dve.wait_ge(s["tp_evac"], 2)
            soft(dve.tensor_scalar(sp[0], lam, -1.0, None, ALU.mult))
            soft(dve.tensor_tensor(sp[1], lam, sp[0], ALU.max))
            dve.wait_ge(s["softp_exp"], 1)
            soft(dve.tensor_scalar(sp[2], sp[1], 2.0, None, ALU.add))
            soft(dve.reciprocal(sp[2], sp[2]))
            soft(dve.tensor_tensor(sp[3], sp[1], sp[2], ALU.mult))
            soft(dve.tensor_tensor(sp[4], sp[3], sp[3], ALU.mult))
            soft(dve.tensor_scalar(sp[5], sp[4], 1.0 / 15, None, ALU.mult))
            for m in (13, 11, 9, 7, 5):
                soft(dve.scalar_tensor_tensor(sp[5], sp[5], 1.0 / m, sp[4], ALU.add, ALU.mult))
            link(dve.scalar_tensor_tensor(sp[5], sp[5], 1.0 / 3, sp[4], ALU.add, ALU.mult))
            link(dve.scalar_tensor_tensor(sp[5], sp[5], 1.0, sp[3], ALU.add, ALU.mult))
            soft(dve.tensor_scalar(sp[0], sp[0], 0.0, -8.0, ALU.max, ALU.mult))
            soft(dve.tensor_scalar(sp[5], sp[5], -16.0, None, ALU.mult))
            soft(dve.tensor_tensor(s8, sp[5], sp[0], ALU.add))
            dve.tensor_copy(xap[:, :, SEG:].rearrange("p c (b j) -> p c b j", b=NB)[:, :, :, 0:CW - 1],
                            chT[:, :, 0:24].rearrange("p c (b j) -> p c b j", b=NB)).then_inc(s["conv_step"], 1)

            def mod(j):
                dve.wait_ge(s["mod_ready"], j + 1)
                dve.tensor_tensor(mods[:, j, :], bank[j % 2][:, 0:P], adab[:, j, :], ALU.add).then_inc(s["mod_evac"], 1)
            dve.wait_ge(s["ld_adab"], 64)
            for j in range(4):
                mod(j)
            for h in range(2):
                dve.tensor_copy(wT[:, 4 * h:4 * h + 4, :], tp_get(f"w{h}")[:, :].rearrange("p (g q) -> p g q", g=4)).then_inc(s["tp_evac"], 1)
            dve.tensor_copy(wsT[0:64], tp_get("ws")[0:64, :].rearrange("p (g q) -> p g q", g=8)).then_inc(s["tp_evac"], 1)

            def scales(sm_gn, gn_count):
                dve.wait_ge(s[sm_gn], gn_count)
                dve.scalar_tensor_tensor(mb[:, 0, 0, :], mb[:, 0, 0, :], 1.0, gn[:, :], ALU.add, ALU.mult).then_inc(s["mod_scaled"], 1)
                dve.scalar_tensor_tensor(mb[0:64, 0, 1, :], mb[0:64, 0, 1, :], 1.0, gn[0:64, :], ALU.add, ALU.mult).then_inc(s["mod_scaled"], 1)

            def normed(t, done, work):
                n = TILES[t][1]
                w = t // 2
                link(dve.scalar_tensor_tensor(work[0:n, :], x[0:n, t, :], rstd[0:n, t:t + 1], mb[0:n, 0, w, :], ALU.mult, ALU.mult))
                dve.tensor_tensor(xn[0:n, t, :].rearrange("t (k p) -> t p k", k=KT), work[0:n, :].rearrange("t (p k) -> t p k", k=KT),
                                  mb[0:n, 1, w, :].rearrange("t (p k) -> t p k", k=KT), ALU.add).then_inc(s[done], 1)

            dve.wait_ge(mods_back[0], 64)
            scales("ld_gn", 16)
            dve.wait_ge(s["rstd_ready"], 1)
            dve.wait_ge(s["mod_scaled"], 2)
            work = dnf[:, 0:D]
            dve.wait_ge(s["acc_zeroed"], 32)
            for t in range(3):
                normed(t, "xn_done", work)
                if t < 2:
                    dve.wait_ge(s["xn_done"], t + 1)

            def xT_get(name, t):
                t0, n = TILES[t]
                for h in range(2):
                    dve.tensor_copy(xT[:, 4 * h:4 * h + 4, t0:t0 + n],
                                    tp_get(f"{name}{t}{h}")[:, :].rearrange("p (k n) -> p k n", k=4)[:, :, 0:n]).then_inc(s["tp_evac"], 1)
            for t in range(3):
                xT_get("x", t)
            dve.wait_ge(s["tp_evac"], TP["x21"] + 1)
            dve.memset(small[:, 60:61], 0.0).then_inc(s["xn_free"], 1)
            dve.wait_ge(s["prj_evac"], CT)
            xas = xap[:, :, SEG:].rearrange("p c (b j) -> p c b j", b=NB)
            xcs = xc[:, :, NPR:].rearrange("p c (b j) -> p c b j", b=NB)
            for k in range(CW):
                for c in range(CT):
                    for dst, src in ((xc[:, c, 0:NPR], xap[:, c, k:k + NPR]), (xcs[:, c], xas[:, c, :, k:k + NT])):
                        wk = chT[:, c, 32 + k:33 + k]
                        if k == 0:
                            ins = dve.tensor_scalar(dst, src, wk, chT[:, c, 36:37], ALU.mult, ALU.add)
                        else:
                            ins = dve.scalar_tensor_tensor(dst, src, wk, dst, ALU.mult, ALU.add)
                        ins.then_inc(s["conv_step"], 1)
                dve.wait_ge(s["conv_step"], 2 + 2 * CT * (k + 1))
            link(dve.tensor_copy(hc[:, :, 9:12], xap[:, :, SEG - 3:SEG]))
            dve.tensor_copy(hc[:, :, 12:36].rearrange("p c (b j) -> p c b j", b=NB), xas[:, :, :, NT:SS]).then_inc(s["conv_done"], 1)
            mod(4)
            mod(5)
            dve.wait_ge(s["expd"], 2 * CT)
            link(dve.tensor_tensor(ii, ii, xc, ALU.mult))
            dve.tensor_scalar(dd, rr, -1.0, 1.0, ALU.mult, ALU.add).then_inc(s["lru_den"], 1)
            dve.wait_ge(s["lru_den"], 1)
            dve.reciprocal(dd, dd).then_inc(s["lru_den"], 1)
            dve.wait_ge(s["lru_den"], 2)
            dve.scalar_tensor_tensor(rr, rr, -2.0, dd, ALU.mult, ALU.mult).then_inc(s["lru_den"], 1)
            mod(6)
            mod(7)
            dve.wait_ge(s["lru_sqrt"], 1)
            link(dve.tensor_tensor(ii, ii, rr, ALU.mult))
            a0 = aa[:, :, NPR:].rearrange("p c (b j) -> p c b j", b=NB)[:, :, :, 0]
            u0 = ii[:, :, NPR:].rearrange("p c (b j) -> p c b j", b=NB)[:, :, :, 0]
            h0 = dd[:, :, 0:NB]
            link(dve.tensor_tensor(h0, a0, chT[:, :, 24:32], ALU.mult))
            link(dve.tensor_tensor(u0, u0, h0, ALU.add))
            link(dve.memset(a0, 0.0))
            link(dve.memset(aa[:, :, 0:1], 0.0))
            link(dve.tensor_tensor_scan(xc.rearrange("p c t -> p (c t)"), aa.rearrange("p c t -> p (c t)"),
                                        ii.rearrange("p c t -> p (c t)"), 0.0, ALU.mult, ALU.add))
            dve.tensor_copy(hc[:, :, 0:1], xc[:, :, NPR - 1:NPR]).then_inc(s["lru_h"], 1)
            dve.tensor_copy(hc[:, :, 1:9], xc[:, :, NPR:].rearrange("p c (b j) -> p c b j", b=NB)[:, :, :, NT - 1]).then_inc(s["lru_h"], 1)
            dve.wait_ge(s["prj_evac"], 2 * CT)
            dve.tensor_tensor(ga, ga, xc, ALU.mult).then_inc(s["ya_sq"], 1)
            dve.wait_ge(s["ya_sq"], 1)
            dve.tensor_tensor(dd, ga, ga, ALU.mult).then_inc(s["ya_sq"], 1)
            mod(8)
            mod(9)
            for c in range(CT):
                dve.tensor_scalar(dd[:, c, :], tp_get(f"g{c}")[:, 0:T], EPS, None, ALU.add).then_inc(s["tp_evac"], 1)
            dve.wait_ge(s["tp_evac"], TP[f"g{CT - 1}"] + 1)
            for c in range(4):
                dve.reciprocal(dd[:, c, :], dd[:, c, :]).then_inc(s["gms_eps"], 1)
            dve.memset(small[:, 61:62], 0.0).then_inc(s["gms_eps"], 1)
            dve.wait_ge(s["gv_sq"], 3)
            for t, (t0, n) in enumerate(TILES):
                dve.tensor_scalar(vrs[0:n, t:t + 1], vss[0:n, t:t + 1], 1.0 / W, EPS, ALU.mult, ALU.add).then_inc(s["v_rs"], 1)
            dve.wait_ge(s["v_rs"], 3)
            link(dve.memset(vrs[64:P, 2:3], 1.0))
            dve.reciprocal(vrs, vrs).then_inc(s["v_rs"], 1)
            dve.wait_ge(s["v_sqrt"], 1)
            dve.wait_ge(s["ld_rows"], 16 * 11)
            for t, (t0, n) in enumerate(TILES):
                dve.scalar_tensor_tensor(vv[0:n, t, :], vv[0:n, t, :], vrs[0:n, t:t + 1], vg_row[0:n, :], ALU.mult, ALU.mult).then_inc(s["v_done"], 1)
            dve.wait_ge(s["gms_sqrt"], 1)
            link(dve.tensor_tensor(ga, ga, dd, ALU.mult))
            mod(10)
            mod(11)
            for c in range(CT):
                for _ in range(4):
                    ins = dve.tensor_scalar(xT[:, c, _ * 80:(_ + 1) * 80], ga[:, c, _ * 80:(_ + 1) * 80], chT[:, c, 40:41], None, ALU.mult)
                    ins.then_inc(s["ya_done"], 1)
            for t, (t0, n) in enumerate(TILES):
                def v3(ap):
                    return ap.rearrange("p (g d) -> p g d", g=8)
                sq = wnat[0:n, 0:4, :].rearrange("p g q -> p (g q)")
                bs = (bsT if t < 2 else bsS)[0:n, :].rearrange("p (g o) -> p g o", o=1).to_broadcast([n, 8, 64])
                st = 7 * t
                uu = us[0:n, t, :]
                dve.tensor_tensor(v3(sq), v3(tp_get(f"s{t}")[0:n, :]), bs, ALU.add).then_inc(s["tp_evac"], 1)
                dve.wait_ge(s["tp_evac"], TP[f"s{t}"] + 1)
                dve.wait_ge(s["prj_evac"], prj_no[("u", t)] + 1)
                dve.tensor_tensor(uu, uu, sq, ALU.mult).then_inc(s["yb_step"], 1)
                dve.wait_ge(s["yb_step"], st + 1)
                dve.tensor_tensor(sq, uu, uu, ALU.mult).then_inc(s["yb_step"], 1)
                dve.wait_ge(s["yb_step"], st + 2)
                gs = small[0:n, 16:24]
                dve.tensor_reduce(gs, v3(sq), AX, ALU.add).then_inc(s["yb_step"], 1)
                dve.wait_ge(s["yb_step"], st + 3)
                dve.tensor_scalar(gs, gs, 1.0 / 64, EPS, ALU.mult, ALU.add).then_inc(s["yb_step"], 1)
                dve.wait_ge(s["yb_step"], st + 4)
                dve.tensor_tensor(uu, uu, og_row[0:n, :], ALU.mult).then_inc(s["yb_step"], 1)
                dve.wait_ge(s["yb_step"], st + 5)
                dve.reciprocal(gs, gs).then_inc(s["yb_step"], 1)
                dve.wait_ge(s["yb_sqrt"], t + 1)
                dve.tensor_tensor(v3(uu), v3(uu), gs.rearrange("p (g o) -> p g o", o=1).to_broadcast([n, 8, 64]), ALU.mult).then_inc(s["yb_step"], 1)
            dve.tensor_copy(hrow[0:36, :], tp_get("hc")[0:36, :]).then_inc(s["tp_evac"], 1)
            dve.wait_ge(s["tp_evac"], TP["hc"] + 1)
            dve.memset(small[:, 62:63], 0.0).then_inc(s["hc_done"], 1)
            for t, (t0, n) in enumerate(TILES):
                dve.tensor_copy(xT[:, 4:8, t0:t0 + n], tp_get(f"y{t}")[:, :].rearrange("p (k n) -> p k n", k=4)[:, :, 0:n]).then_inc(s["tp_evac"], 1)
            dve.memset(small[:, 63:64], 0.0).then_inc(s["mix_free"], 1)
            dve.wait_ge(mods_back[1], 32)
            work = sqy2 = et[:, 4096:4096 + D]
            for t, (t0, n) in enumerate(TILES):
                for c in range(2):
                    q = 2 * t + c
                    dve.wait_ge(s["wout_ready"], q + 1)
                    wk = work[0:n, c * HALF:(c + 1) * HALF]
                    link(dve.tensor_tensor(wk, bank[WO_BANK[q]][0:n, :], gmod[0:n, t // 2, c * HALF:(c + 1) * HALF], ALU.mult))
                    if c == 0:
                        link(dve.tensor_tensor(x[0:n, t, 0:HALF], x[0:n, t, 0:HALF], wk, ALU.add))
                    else:
                        dve.tensor_tensor(x[0:n, t, HALF:D], x[0:n, t, HALF:D], wk, ALU.add).then_inc(s["x2_done"], 1)
            dve.wait_ge(s["x2_done"], 3)
            dve.wait_ge(mods_back[2], 64)
            scales("gn_ffn", 16)
            dve.wait_ge(s["mod_scaled"], 4)
            for t, (t0, n) in enumerate(TILES):
                dve.wait_ge(s["x2_sq"], t + 1)
                dve.tensor_scalar(rstd[0:n, t:t + 1], ssq[0:n, t:t + 1], 1.0 / D, EPS, ALU.mult, ALU.add).then_inc(s["rs2_in"], 1)
                dve.wait_ge(s["rs2_in"], 2 * t + 1)
                dve.reciprocal(rstd[0:n, t:t + 1], rstd[0:n, t:t + 1]).then_inc(s["rs2_in"], 1)
                dve.wait_ge(s["rs2"], t + 1)
                if t == 0:
                    dve.wait_ge(s["v_out"], 16)
                normed(t, "xn_ready", work)
                dve.wait_ge(s["xn_ready"], t + 1)
            for t in range(3):
                xT_get("z", t)
            dve.memset(score[64:P, 2, :], 0.5).then_inc(s["pad_set"], 1)
            dve.memset(pos[64:P, 2, :], 0.0).then_inc(s["pad_set"], 1)
            def over_e(ap):
                return ap.rearrange("p (t o) -> p t o", o=1).to_broadcast([P, 3, NE])
            dve.wait_ge(s["sc_done"], 3)
            dve.wait_ge(s["ld_router"], 32)
            link(dve.tensor_tensor(biased, score, rbias[:, :].rearrange("p (o e) -> p o e", o=1).to_broadcast([P, 3, NE]), ALU.add))
            for t in range(3):
                dve.max(top[:, t, :], biased[:, t, :]).then_inc(s["route_step"], 1)
            dve.wait_ge(s["route_step"], 3)
            for t in range(3):
                dve.match_replace(rest[:, t, :], top[:, t, :], biased[:, t, :], -3.0e38).then_inc(s["route_step"], 1)
            dve.wait_ge(s["route_step"], 6)
            dve.tensor_scalar(mask, rest, -3.0e38, None, ALU.is_equal).then_inc(s["mask_done"], 1)
            dve.memset(small[:, 59:60], 0.0).then_inc(s["tp_evac"], 1)
            dve.wait_ge(s["mask_done"], 1)
            link(dve.tensor_tensor(score, score, mask, ALU.mult))
            link(dve.tensor_reduce(rsc[:, 0:3], score, AX, ALU.add))
            link(dve.reciprocal(rsc[:, 0:3], rsc[:, 0:3]))
            link(dve.tensor_scalar(rsc[:, 0:3], rsc[:, 0:3], 2.5, None, ALU.mult))
            link(dve.tensor_tensor(gpart, score, over_e(rsc[:, 0:3]), ALU.mult))
            link(dve.tensor_copy(tg[:, :, :, 1, 0], gpart))
            link(dve.tensor_tensor(gpart, gpart, tg[:, :, :, 1, 0], ALU.subtract))
            link(dve.tensor_copy(tg[:, :, :, 1, 1], gpart))
            link(dve.tensor_tensor(gpart, gpart, tg[:, :, :, 1, 1], ALU.subtract))
            dve.tensor_copy(tg[:, :, :, 1, 2], gpart).then_inc(s["route_step"], 1)
            link(dve.tensor_copy(tg[:, :, :, 0, 0], over_e(tokc[:, :])))
            link(dve.tensor_tensor(rsc[:, 3:6], tokc[:, :], tg[:, :, 0, 0, 0], ALU.subtract))
            dve.tensor_copy(tg[:, :, :, 0, 1], over_e(rsc[:, 3:6])).then_inc(s["route_step"], 1)
            dve.memset(tg[:, :, :, 0, 2], 0.0).then_inc(s["route_step"], 1)
            b = tp_get("pos")
            for t, (t0, n) in enumerate(TILES):
                dve.scalar_tensor_tensor(pos[0:n, t, :], b[0:n, t * NE:(t + 1) * NE], 1.0, mask[0:n, t, :], ALU.add, ALU.mult).then_inc(s["route_step"], 1)
            dve.wait_ge(s["route_step"], 12)
            link(dve.tensor_scalar(pos, pos, -1.0, None, ALU.add))
            link(dve.tensor_reduce(cmax, b[:, 3 * NE:4 * NE], AX, ALU.max))
            link(dve.tensor_copy(cnt_i[:, NE:NE + 1], cmax))
            dve.tensor_copy(cnt_i[:, 0:NE], b[:, 3 * NE:4 * NE]).then_inc(s["tp_evac"], 1)
            dve.wait_ge(s["tp_evac"], TP["pos"] + 1)
            dve.memset(small[:, 58:59], 0.0).then_inc(s["flags"], 1)
            for t, (t0, n) in enumerate(TILES):
                dve.wait_ge(s["sh_act"], t + 1)
                if t:
                    dve.wait_ge(s["tp_ready"], TP[f"h{t - 1}"] + 1)
                dve.tensor_tensor(shid[0:n, :].rearrange("t (j p) -> t p j", j=2), sgs[0:n, :].rearrange("t (p j) -> t p j", j=2),
                                  bank[4 + t][0:n, FE:2 * FE].rearrange("t (p j) -> t p j", j=2), ALU.mult).then_inc(s["sh_hid"], 1)
                dve.tensor_copy(shT[:, :, 0:n], tp_get(f"h{t}")[:, 0:2 * P].rearrange("p (j n) -> p j n", j=2)[:, :, 0:n]).then_inc(s["tp_evac"], 1)

            def select(r, i, u):
                e = r * NE + i * U + u
                if not (isinstance(e, int) and e == 0):
                    dve.wait_ge(s["sel_ready"], e)
                for t, (t0, n) in enumerate(TILES):
                    ins = dve.tensor_scalar(sel[0:n, t, :], iota_s[0:n, :], pos[0:n, t, bass.ds(i * U + u, 1)], None, ALU.is_equal)
                ins.then_inc(s["sel_built"], 1)

            def index(r, i, u):
                e = r * NE + i * U + u
                dve.wait_ge(s["sel_ready"], e + 1)
                if not (isinstance(e, int) and e < U):
                    for b in range(2):
                        dve.wait_ge(scattered[b], 16 * e - 16 * (U - 1))
                dve.tensor_reduce(pick_out[:, u], bank[7][:, 0:12].rearrange("p (b c m) -> p b c m", b=2, c=2), AX, ALU.add)\
                   .then_inc(s["gate_ready"], 1)
                dve.wait_ge(s["gate_ready"], e + 1)
                dve.tensor_scalar(idx[:, u, :], pick_out[:, u, :, 0], halfc[:, 0:1], None, ALU.add).then_inc(s["idx_ready"], 1)

            def xt0(r, i, u):
                dve.wait_ge(s["xt_ready"], r * NE + i * U + u + 1)
                dve.tensor_copy(xt[:, 0].rearrange("p k h n -> p (k h n)"), bank[2][:, :]).then_inc(s["xt0_evac"], 1)

            def hidden(r, i, u):
                e = r * NE + i * U + u
                dve.wait_ge(s["up_evac"], e + 1)
                if not (isinstance(e, int) and e == 0):
                    dve.wait_ge(s["ht_ready"], e)
                dve.tensor_tensor(hid[0:64].rearrange("t b j p -> t b p j"), sg[0:64, :].rearrange("t (b p j) -> t b p j", b=2, j=2),
                                  up[0:64, :].rearrange("t (b p j) -> t b p j", b=2, j=2), ALU.mult).then_inc(s["hid_ready"], 1)

            def ht(r, i, u):
                dve.wait_ge(s["ht_ready"], r * NE + i * U + u + 1)
                if not (isinstance(i, int) and i == 0 and u == 0 and r == 0):
                    dve.wait_ge(s["y_ready"], r * NE + i * U + u)
                dve.tensor_copy(hT.rearrange("p b j n -> p (b j n)"), bank[4][:, 0:256]).then_inc(s["ht_evac"], 1)

            def y0(r, i, u):
                e = r * NE + i * U + u
                dve.wait_ge(s["y_ready"], e + 1)
                if not (isinstance(e, int) and e < 2):
                    dve.wait_ge(scattered[0], 16 * e - 16)
                dve.tensor_scalar(yo[:, u % 2, 0, :], bank[5][:, :], pick_out[:, u, 0, 1:2], None, ALU.mult).then_inc(s["y0_evac"], 1)

            def body(r, i, first=False, last=False):
                for u in range(U):
                    before = (r, i if u else i - 1, (u - 1) % U)
                    if not (last and u >= U - 2):
                        select(r, i + (u + 2) // U, (u + 2) % U)
                    if not (first and u == 0):
                        ht(*before)
                    if not (last and u >= U - 2):
                        index(r, i + (u + 2) // U, (u + 2) % U)
                    if not (last and u == U - 1):
                        xt0(r, i + (u + 1) // U, (u + 1) % U)
                    hidden(r, i, u)
                    if not (first and u == 0):
                        y0(*before)

            def rounds(r):
                select(r, 0, 0)
                index(r, 0, 0)
                select(r, 0, 1)
                index(r, 0, 1)
                xt0(r, 0, 0)
                body(r, 0, first=True)
                if r == 0:
                    dve.wait_ge(g_back, 32)
                    dve.wait_ge(s["sh_evac"], 6)
                    for t, (t0, n) in enumerate(TILES):
                        link(dve.tensor_tensor(sh[0:n, t, :], sh[0:n, t, :], gmod[0:n, t // 2, :], ALU.mult))
                        dve.tensor_tensor(x[0:n, t, :], x[0:n, t, :], sh[0:n, t, :], ALU.add).then_inc(s["pre_done"], 1)
                with dve.Fori(1, NE // U - 1) as i:
                    body(r, i)
                body(r, NE // U - 1, last=True)
                ht(r, NE // U - 1, U - 1)
                y0(r, NE // U - 1, U - 1)

            def out(t):
                n = TILES[t][1]
                dve.wait_ge(s["fin_rs"], 2 * t + 1)
                dve.tensor_scalar(frs[0:n, t:t + 1], fss[0:n, t:t + 1], 1.0 / D, EPS, ALU.mult, ALU.add).then_inc(s["rs_in"], 1)
                dve.wait_ge(s["rs_in"], 4 + 2 * t + 1)
                dve.reciprocal(frs[0:n, t:t + 1], frs[0:n, t:t + 1]).then_inc(s["rs_in"], 1)
                dve.wait_ge(s["fin_rs"], 2 * t + 2)
                dve.scalar_tensor_tensor(xn[0:n, t, :], xn[0:n, t, :], frs[0:n, t:t + 1], gn[0:n, :], ALU.mult, ALU.mult).then_inc(s["out_done"], 1)

            rounds(0)
            most = dve.value_load(cnt_i[0:1, NE:NE + 1], min_val=0, max_val=T)
            for r in range(1, ROUNDS):
                with dve.If(most > r * ROUND):
                    for t, (t0, n) in enumerate(TILES):
                        dve.tensor_scalar(pos[0:n, t, :], pos[0:n, t, :], -float(ROUND), None, ALU.add).then_inc(s["pos_shifted"], 1)
                    dve.wait_ge(s["pos_shifted"], 3 * r)
                    rounds(r)
            dve.wait_ge(s["gn_fin"], 16)
            for t, (t0, n) in enumerate(TILES):
                w = xn[0:n, t, :]
                dve.wait_ge(acc_back[t], 32)
                dve.tensor_tensor(w, w, sh[0:n, t, :], ALU.add).then_inc(s["fin_sq"], 1)
                dve.wait_ge(s["fin_sq"], 3 * t + 1)
                dve.tensor_tensor(w, w, gmod[0:n, t // 2, :], ALU.mult).then_inc(s["fin_sq"], 1)
                dve.wait_ge(s["fin_sq"], 3 * t + 2)
                dve.tensor_tensor(w, w, x[0:n, t, :], ALU.add).then_inc(s["fin_sq"], 1)
                if t:
                    out(t - 1)
            out(2)


_INS = ["x_prompt", "x_sample", "c_prompt", "c_sample", "state_lru_h", "state_conv", "ada_w", "ada_b", "norm_mix_g",
        "norm_ffn_g", "w_in", "conv_w", "conv_b", "gate_r_w", "gate_r_b", "gate_i_w", "gate_i_b", "lru_lambda",
        "sgu_norm_g", "sgu_w", "sgu_b", "out_norm_g", "w_out", "router_w", "router_bias", "exp_w_gate", "exp_w_up",
        "exp_w_down", "shared_w_gate", "shared_w_up", "shared_w_down", "final_norm_g"]
_OUTS = [("y_prompt", (1, NPR, D)), ("y_sample", (NB, NT, D)), ("h_prompt", (1, 1, W)), ("conv_prompt", (1, 1, CW - 1, W)),
         ("h_sample", (1, NB, W)), ("conv_sample", (1, NB, CW - 1, W)), ("v_sample", (1, NB, NT, W))]


def kernel(**inputs):
    import numpy as np
    import concourse.bacc as bacc
    from concourse.bass_utils import run_bass_kernel_spmd as run

    nc = bacc.Bacc("TRN2", target_bir_lowering=False, num_devices=1)
    arrays, io = {}, {}
    for name in _INS:
        a = np.ascontiguousarray(inputs[name])
        arrays[f"in_{name}"] = a
        io[name] = nc.dram_tensor(f"in_{name}", a.shape, mybir.dt.from_np(a.dtype), kind="ExternalInput").ap()
    for name, shape in _OUTS:
        io[name] = nc.dram_tensor(f"out_{name}", shape, F32, kind="ExternalOutput").ap()
    build(nc, io)
    r = run(nc, [arrays], core_ids=[0])
    return tuple(r.results[0][f"out_{name}"] for name, _ in _OUTS)
```

```python
from contextlib import ExitStack

import concourse.bass as bass
from concourse import mybir

F32 = mybir.dt.float32
U32 = mybir.dt.uint32
BF16 = mybir.dt.bfloat16
I32 = mybir.dt.int32
ALU = mybir.AluOpType
ACT = mybir.ActivationFunctionType
AX = mybir.AxisListType.X

P = 128
D = 1024
KT = D // P
NPR = 256
NB, NT = 8, 8
T = NPR + NB * NT
TILES = [(0, 128), (128, 128), (256, 64)]
W = 512
CW = 4
CT = W // P
NE = 64
FE = 256
NSEQ = 9
EPS = 1e-6
HALF = D // 2
OOB = 2 * D
SLOTS = 4
U = 8
ROUND = 128
ROUNDS = -(-T // ROUND)
SEG = NPR + CW - 1
SS = NT + CW - 1


def build(nc, io):
    with ExitStack() as ctx:
        ctx.enter_context(nc.allow_non_contiguous_dma(reason="small transposed bias rows"))

        def sb(name, shape, dt=F32):
            return ctx.enter_context(nc.sbuf_tensor(name, shape, dt))

        def sem(name):
            return ctx.enter_context(nc.semaphore(name))

        xn_rows = nc.dram_tensor("xn_rows", [T, D], F32).ap()
        acc_rows = [nc.dram_tensor(f"acc_rows{b}", [2 * T, HALF], F32).ap() for b in range(2)]
        xn_half = xn_rows.rearrange("t (h n) -> (t h) n", h=2)

        gu = [sb(f"gu{s}", [P, KT, 512]) for s in range(SLOTS)]
        dn = sb("dn", [P, SLOTS, 2 * D])
        x = sb("x", [P, 3, D])
        xn = sb("xn", [P, 3, D])
        xT = sb("xT", [P, KT, T])
        mb = sb("mb", [P, 2, 2, D])
        gmod = sb("gmod", [P, 2, D])
        gn = sb("gn", [P, D])
        sh = sb("sh", [P, 3, D])
        et = sb("et", [P, 7296])
        ident = sb("ident", [P, P])
        ones = sb("ones", [P, P])
        upper = sb("upper", [P, P])
        blk = sb("blk", [P, P])
        cT = sb("cT", [P, KT, 32])
        chT = sb("chT", [P, CT, 41])
        small = sb("small", [P, 64])
        wrt = sb("wrt", [P, KT, NE])
        rbias = sb("rbias", [P, NE])
        iota_s = sb("iota_s", [P, 256])
        spread_s = iota_s[:, :].rearrange("p (g n) -> p g n", g=4)
        tokc = sb("tokc", [P, 3])
        halfc = sb("halfc", [P, 1])
        cnt_i = sb("cnt_i", [P, NE + 1], I32)
        idx = sb("idx", [P, U, 2], U32)
        pick_out = sb("pick_out", [P, U, 2, 2])
        hc = sb("hc", [P, CT, 36])

        dnf = dn[:, :, :].rearrange("p s n -> p (s n)")

        def lru(n):
            return dnf[:, n * 1280:(n + 1) * 1280].rearrange("p (c t) -> p c t", c=CT)
        xc, rr, aa, ii, dd, ga = (lru(n) for n in range(6))
        chrow = dnf[:, 7680:8192]
        o = [0]

        def part(n):
            o[0] += n
            return et[:, o[0] - n:o[0]]
        xap = part(CT * (SEG + NB * SS)).rearrange("p (c t) -> p c t", c=CT)
        wnat = part(1024).rearrange("p (g q) -> p g q", g=8)
        wT = part(1024).rearrange("p (g q) -> p g q", g=8)
        wsn = part(512).rearrange("p (g q) -> p g q", g=8)
        wsT = part(512).rearrange("p (g q) -> p g q", g=8)
        vg_row = part(512)
        og_row = part(512)
        mods = part(12 * P).rearrange("p (j n) -> p j n", j=12)
        bsT = part(8)
        bsS = part(8)
        assert o[0] <= 7296
        shf = sh[:, :, :].rearrange("p t n -> p (t n)")
        wr = shf[:, 0:512].rearrange("p (c j) -> p c j", c=CT)
        wi = shf[:, 512:1024].rearrange("p (c j) -> p c j", c=CT)
        adab = shf[:, 1024:2560].rearrange("p (j n) -> p j n", j=12)
        hrow = shf[:, 2560:3072]
        xnf = xn[:, :, :].rearrange("p t n -> p (t n)")
        us = xnf[:, 0:1536].rearrange("p (t n) -> p t n", t=3)
        vv = xnf[:, 1536:3072].rearrange("p (t n) -> p t n", t=3)
        crow = gmod[0:NSEQ, 0, :]
        o[0] = 0
        xg = part(2048).rearrange("p (b s n) -> p b s n", b=2, s=2)
        xt = part(1024).rearrange("p (s k h n) -> p s k h n", s=2, k=4, h=2)
        sg = part(512)
        up = part(512)
        hid_f = part(512)
        hid = hid_f.rearrange("p (s j f) -> p s j f", s=2, j=2)
        hT = part(256).rearrange("p (s j n) -> p s j n", s=2, j=2)
        sel = part(384).bitcast(BF16).rearrange("p (t n) -> p t n", t=3)
        yo = part(2048).rearrange("p (a s n) -> p a s n", a=2, s=2)
        xs_pre = dnf[0:64, 5120:5120 + D]
        shid = et[:, o[0] - 768:o[0] - 512]
        shT = et[:, o[0] - 512:o[0] - 256].rearrange("p (j n) -> p j n", j=2)
        sgs = et[:, o[0] - 256:o[0]]
        up_s = hid_f[0:64, 0:FE]
        wo_hi = hid_f[0:64, :]
        sqy = et[:, 3072:4096]
        assert o[0] <= 7296
        mbf = mb[:, :, :, :].rearrange("p a b n -> p (a b n)")
        score = mbf[:, 0:192].rearrange("p (t e) -> p t e", t=3)
        biased = mbf[:, 192:384].rearrange("p (t e) -> p t e", t=3)
        rest = mbf[:, 384:576].rearrange("p (t e) -> p t e", t=3)
        mask = mbf[:, 576:768].rearrange("p (t e) -> p t e", t=3)
        pos = mbf[:, 768:960].rearrange("p (t e) -> p t e", t=3)
        top = mbf[:, 960:984].rearrange("p (t e) -> p t e", t=3)
        tg = mbf[:, 1440:1440 + 576].bitcast(BF16).rearrange("p (t e c m) -> p t e c m", t=3, c=2, m=3)
        gpart = mbf[:, 2048:2240].rearrange("p (t e) -> p t e", t=3)
        cmax = mbf[:, 1400:1401]
        rsc = mbf[:, 1408:1420]

        bank = [ctx.enter_context(nc.psum_tensor(f"bank{b}", [P, 512], F32)) for b in range(8)]

        names = """v_out consts consts_v cT_zero blk_zero ld_c ld_x ld_ch ld_adab ld_gn ld_rg ld_sgu ld_wsn ld_rows
            ld_router acc_zeroed zero_ready csilu tp_ready tp_evac mod_ready mod_evac sumsq sumsq_v rs_in rstd_ready
            bc_ready bc_evac_v bc_evac_a gm_in gf_ready gf_in up_moved wo_moved mod_scaled xn_done xn_done_s
            xn_ready xn_free prj_ready prj_evac conv_step conv_done softp softp_exp expd lru_den lru_sqrt lru_h
            ya_sq gms_eps gms_sqrt ya_done msk gv_sq v_rs v_sqrt v_done yb_step yb_sqrt out_small wout_ready x2_done
            x2_sq rs2_in rs2 sc_done route_step routed logit_done mask_done tok_written sh_ready sh_act sh_hid
            sh_down_ready sh_evac xg_zero adab_zero fin_pool code_in lru_asq spread_in iota_in table_in h_ready
            h_evac x_pre pool_step gelu_half sel_built sel_ready idx_ready gate_ready xt_ready xt0_evac xt1_evac
            gu_done sg_evac up_evac hid_ready ht_ready ht_evac y_ready y0_evac y1_evac pool_go pad_set pos_shifted
            flags fin_step pre_done fin_sq fin_rs out_done gn_ffn gn_fin hc_done mix_free""".split()
        s = {n: sem(n) for n in names}
        ld_piece = [sem(f"ld_piece{i}") for i in range(SLOTS)]
        ld_gu = [sem(f"ld_gu{i}") for i in range(SLOTS)]
        ld_dn = [sem(f"ld_dn{i}") for i in range(SLOTS)]
        ld_shared_gu, ld_shared_dn = sem("ld_shared_gu"), sem("ld_shared_dn")
        gathered = [sem("gathered0"), sem("gathered1")]
        gathered2 = [sem("gathered2_0"), sem("gathered2_1")]
        scattered = [sem("scattered0"), sem("scattered1")]
        acc_back = [sem(f"acc_back{t}") for t in range(3)]
        dve_link, act_link = sem("dve_link"), sem("act_link")

        ada_p = io["ada_w"][0].rearrange("(p k) (j n) -> j p k n", k=KT, n=512)
        win_p = io["w_in"][0].rearrange("(p k) (j n) -> j p k n", k=KT, n=512)
        wout_p = io["w_out"][0].rearrange("(k p) (j n) -> j p k n", p=P, n=512)
        eg = io["exp_w_gate"][0].rearrange("e (p k) f -> e p k f", k=KT)
        eu = io["exp_w_up"][0].rearrange("e (p k) f -> e p k f", k=KT)
        ed = io["exp_w_down"][0].rearrange("e (p j) n -> e p (j n)", j=2)

        PIECES = ([("ada", j) for j in range(4)] + [("in", 0), ("ada", 4), ("ada", 5), ("in", 1), ("ada", 6), ("ada", 7),
                  ("in", 3), ("ada", 8), ("ada", 9), ("in", 2), ("ada", 10), ("ada", 11), ("out", 0), ("out", 1)])
        NP = len(PIECES)
        piece_no = {pc: n for n, pc in enumerate(PIECES)}
        SH_NO = NP
        E_NO = NP + 1
        SH_SLOT = SH_NO % SLOTS

        def used(n):
            if n == SH_NO:
                return s["sh_ready"], 3
            kind, j = PIECES[n]
            if kind == "ada":
                return s["mod_ready"], j + 1
            if kind == "in":
                return s["prj_ready"], prj_no[[("xa", CT - 1), ("ga", CT - 1), ("u", 2), ("v", 2)][j]] + 1
            return s["wout_ready"], 5

        def gslot(u):
            return (E_NO + u) % SLOTS

        def dslot(u):
            return (1 + u) % SLOTS

        TP = {}
        for n in (["c"] + [f"x{t}{h}" for t in range(3) for h in range(2)] + ["ch", "w0", "w1", "ws"]
                  + [f"g{c}" for c in range(CT)] + ["s0", "s1", "s2", "y0", "y1", "y2", "hc"]
                  + [f"z{t}{h}" for t in range(3) for h in range(2)] + ["pos"]):
            TP[n] = len(TP)

        def tp_bank(n):
            return bank[2 + TP[n] % 2]

        PRJ = ([("xa", c) for c in range(CT)] + [("ga", c) for c in range(CT)] + [("r", c) for c in range(CT)]
               + [("i", c) for c in range(CT)] + [("gm", g) for g in range(4)] + [("v", t) for t in range(3)]
               + [("fp", g) for g in range(4)] + [("u", t) for t in range(3)] + [("fs", g) for g in range(4)])
        prj_no = {n: i for i, n in enumerate(PRJ)}

        def prj_bank(n):
            return bank[4 + prj_no[n] % 4]
        WO_BANK = [4, 5, 6, 1, 0]
        GF_BANK = [1, 0, 6, 1]

        spare = small[:, 60:61]
        FIN_ORDER = (0, 2, 1)

        rstd = small[:, 0:3]
        ssq = small[:, 3:6]
        vss = small[:, 6:9]
        vrs = small[:, 9:12]
        s8 = small[:, 12:16]
        lam = chT[:, :, 39]
        sp = [small[:, 16 + 4 * n:20 + 4 * n] for n in range(8)]
        fss = small[:, 52:55]
        skipped = small[0:1, 16:16 + 2 * U]
        frs = small[:, 55:58]

        def mb_view(w, g):
            return mb[0:P if w == 0 else 64, :, w, :].rearrange("p a (j g n) -> p a j g n", j=2, g=4)[:, :, :, g, :]

        def gmod_view(w, g):
            return gmod[0:P if w == 0 else 64, w, :].rearrange("p (j g n) -> p j g n", j=2, g=4)[:, :, g, :]

        def bc_view(b, n):
            return bank[b][0:n, :].rearrange("p (a j n) -> p a j n", a=2, j=2)

        block = ctx.enter_context(nc.Block())

        @block.sync
        def _(sync):
            sync.dma_start(crow[0:1, :], io["c_prompt"]).then_inc(s["ld_c"], 16)
            sync.dma_start(crow[1:NSEQ, :], io["c_sample"]).then_inc(s["ld_c"], 16)
            for n, (kind, j) in enumerate(PIECES):
                if n == 1:
                    bsrc = io["ada_b"].rearrange("o (j g n) -> o j g n", j=12, g=4)
                    sync.wait_ge(s["adab_zero"], 1)
                    for g in range(4):
                        sync.dma_start(adab[32 * g:32 * g + NSEQ], bsrc[:, :, g, :].to_broadcast([NSEQ, 12, P])).then_inc(s["ld_adab"], 16)
                    sync.dma_start(x[:, 0:2, :], io["x_prompt"][0].rearrange("(t p) n -> p t n", p=P)).then_inc(s["ld_x"], 16)
                    sync.dma_start(x[0:64, 2, :], io["x_sample"].rearrange("b t n -> (b t) n")).then_inc(s["ld_x"], 16)
                if n == 3:
                    sync.dma_start(gn[:, :], io["norm_mix_g"].to_broadcast([P, D])).then_inc(s["ld_gn"], 16)
                if n == 5:
                    sync.wait_ge(s["zero_ready"], 1)
                    for b in range(2):
                        sync.dma_start(acc_rows[b].rearrange("(p a) n -> p (a n)", p=P), dnf[:, 0:2560]).then_inc(s["acc_zeroed"], 16)
                if n >= SLOTS:
                    sync.wait_ge(*used(n - SLOTS))
                src = {"ada": ada_p, "in": win_p, "out": wout_p}[kind][j]
                sync.dma_start(gu[n % SLOTS][:, :, :], src).then_inc(ld_piece[n % SLOTS], 16)
            sync.wait_ge(*used(SH_NO - SLOTS))
            for c, name in enumerate(("shared_w_gate", "shared_w_up")):
                sync.dma_start(gu[SH_SLOT][:, :, c * FE:(c + 1) * FE],
                               io[name][0].rearrange("(p k) f -> p k f", k=KT)).then_inc(ld_shared_gu, 16)

            def load_gu(r, i, u):
                g = r * NE + i * U + u
                if isinstance(g, int) and g < SLOTS:
                    sync.wait_ge(*used(E_NO + g - SLOTS))
                else:
                    sync.wait_ge(s["gu_done"], g - (SLOTS - 1))
                e = i * U + u
                sync.dma_start(gu[gslot(u)][:, :, 0:FE], eg[e]).then_inc(ld_gu[gslot(u)], 16)
                sync.dma_start(gu[gslot(u)][:, :, FE:2 * FE], eu[e]).then_inc(ld_gu[gslot(u)], 16)

            def load_dn(r, i, u):
                g = r * NE + i * U + u
                if isinstance(g, int) and g == SLOTS - 1:
                    sync.wait_ge(s["sh_down_ready"], 5)
                elif not (isinstance(g, int) and g < SLOTS):
                    sync.wait_ge(s["y_ready"], g - (SLOTS - 1))
                sync.dma_start(dn[:, dslot(u), :], ed[i * U + u]).then_inc(ld_dn[dslot(u)], 16)

            def back(i, u):
                return (i, u - 1) if u else (i - 1, U - 1)

            for u in range(3):
                load_gu(0, 0, u)
            sync.wait_ge(s["ya_done"], CT)
            sync.wait_ge(s["mix_free"], 1)
            sync.dma_start(dn[:, 0, :], io["shared_w_down"][0].rearrange("(p j) n -> p (j n)", j=2)).then_inc(ld_shared_dn, 16)
            for u in range(2):
                load_dn(0, 0, u)
            load_gu(0, 0, 3)
            load_dn(0, 0, 2)
            load_gu(0, 0, 4)
            for u in range(5, U):
                load_gu(0, 0, u)
                load_dn(0, 0, u - 2)
            load_dn(0, 0, U - 2)
            with sync.Fori(1, NE // U) as i:
                for u in range(U):
                    load_gu(0, i, u)
                    load_dn(0, *back(i, u))
            load_dn(0, NE // U - 1, U - 1)
            sync.wait_ge(s["flags"], 1)
            most = sync.value_load(cnt_i[0:1, NE:NE + 1], min_val=0, max_val=T)
            for r in range(1, ROUNDS):
                with sync.If(most > r * ROUND):
                    for u in range(U):
                        load_gu(r, 0, u)
                        if u:
                            load_dn(r, 0, u - 1)
                    with sync.Fori(1, NE // U) as i:
                        for u in range(U):
                            load_gu(r, i, u)
                            load_dn(r, *back(i, u))
                    load_dn(r, NE // U - 1, U - 1)
            sync.wait_ge(s["routed"], 1)
            sync.wait_ge(s["pre_done"], 3)
            for t, (t0, n) in (2, TILES[2]), (0, TILES[0]), (1, TILES[1]):
                for b, dst in ((0, xn), (1, sh)):
                    sync.dma_start(dst[0:n, t, :], acc_rows[b][2 * t0:2 * (t0 + n), :].rearrange("(p h) n -> p (h n)", h=2)).then_inc(acc_back[t], 16)
            for turn, t in enumerate(FIN_ORDER):
                t0, n = TILES[t]
                sync.wait_ge(s["out_done"], turn + 1)
                dst = io["y_prompt"][0, t0:t0 + n, :] if t < 2 else io["y_sample"].rearrange("b t n -> (b t) n")
                sync.dma_start(dst, xn[0:n, t, :]).then_inc(s["fin_step"], 16)
            sync.wait_ge(s["fin_step"], 48)
            sync.wait_ge(s["out_small"], 64)
            sync.wait_ge(s["v_out"], 16)

        @block.gpsimd
        def _(pool):
            pool.memset(ident[:, :], 0.0).then_inc(s["consts"], 1)
            pool.memset(ones[:, :], 1.0).then_inc(s["consts"], 1)
            pool.memset(upper[:, :], 1.0).then_inc(s["consts"], 1)
            pool.wait_ge(s["consts"], 3)
            pool.affine_select(out=ident[:, :], in_=ident[:, :], compare_op=ALU.not_equal, fill=1.0, base=0,
                               pattern=[[-1, P]], channel_multiplier=1).then_inc(s["consts"], 1)
            pool.affine_select(out=upper[:, :], in_=upper[:, :], compare_op=ALU.is_gt, fill=0.0, base=0,
                               pattern=[[1, P]], channel_multiplier=-1).then_inc(s["consts"], 1)
            pool.iota(tokc[:, :], allow_small_or_imprecise_dtypes=True, pattern=[[2 * P, 3]], base=-OOB, channel_multiplier=2).then_inc(s["consts"], 1)
            pool.wait_ge(s["x_pre"], 3)
            pool.wait_ge(s["bc_evac_a"], 4)
            sc1 = mb[0:64, 1, 1, :]
            pool.tensor_tensor(sc1, sc1, xs_pre, ALU.mult).then_inc(s["pool_step"], 1)
            pool.wait_ge(s["pool_step"], 1)
            pool.tensor_tensor(xs_pre, xs_pre, sc1, ALU.add).then_inc(s["pool_step"], 1)
            pool.wait_ge(s["pool_step"], 2)
            pool.tensor_tensor(xn[0:64, 2, :].rearrange("t (k p) -> t p k", k=KT), xs_pre.rearrange("t (p k) -> t p k", k=KT),
                               mb[0:64, 0, 1, :].rearrange("t (p k) -> t p k", k=KT), ALU.add).then_inc(s["xn_done_s"], 1)
            pool.wait_ge(s["ld_sgu"], 16)
            pool.affine_select(out=wnat, in_=wnat, compare_op=ALU.is_ge, fill=0.0, base=0,
                               pattern=[[0, 8], [-1, P]], channel_multiplier=1).then_inc(s["msk"], 1)
            pool.wait_ge(s["ld_wsn"], 16 * NB)
            pool.affine_select(out=wsn[0:64, :, :], in_=wsn[0:64, :, :], compare_op=ALU.is_ge, fill=0.0, base=0,
                               pattern=[[0, 8], [-1, 64]], channel_multiplier=1).then_inc(s["msk"], 1)

            pool.wait_ge(s["v_done"], 3)
            pool.dma_start(io["v_sample"].rearrange("o b t n -> (o b t) n"), vv[0:64, 2, :]).then_inc(s["v_out"], 16)
            pool.wait_ge(s["hc_done"], 1)
            pool.dma_start(io["h_prompt"].rearrange("o b n -> (o b) n"), hrow[0:1, :]).then_inc(s["out_small"], 16)
            pool.dma_start(io["h_sample"].rearrange("o b n -> (o b) n"), hrow[1:9, :]).then_inc(s["out_small"], 16)
            pool.dma_start(io["conv_prompt"].rearrange("o b j n -> (o b j) n"), hrow[9:12, :]).then_inc(s["out_small"], 16)
            pool.dma_start(io["conv_sample"].rearrange("o b j n -> (o b j) n"), hrow[12:36, :]).then_inc(s["out_small"], 16)
            pool.wait_ge(s["mix_free"], 1)
            pool.memset(et[:, 0:2048], 0.0).then_inc(s["xg_zero"], 1)
            for t, (t0, n) in enumerate(TILES):
                pool.wait_ge(s["xn_ready"], t + 1)
                pool.dma_start(xn_rows[t0:t0 + n, :], xn[0:n, t, :]).then_inc(s["tok_written"], 16)
            pool.wait_ge(s["gf_ready"], 4)
            pool.iota(iota_s[:, :], allow_small_or_imprecise_dtypes=True, pattern=[[64, 2], [0, 2], [1, 64]], base=0, channel_multiplier=0).then_inc(s["iota_in"], 1)
            pool.wait_ge(s["tok_written"], 48)
            pool.wait_ge(s["xg_zero"], 1)
            pool.wait_ge(s["acc_zeroed"], 32)

            def is_full(r, i, u):
                return pool.value_load(cnt_i[0:1, bass.ds(i * U + u, 1)], min_val=0, max_val=T) > (r * ROUND + 64)

            def gather(r, i, u):
                e = r * NE + i * U + u
                full = is_full(r, i, u)
                pool.wait_ge(s["idx_ready"], e + 1)
                if not (isinstance(e, int) and e < 2):
                    pool.wait_ge(s["xt_ready"], e - 1)
                pool.sem_inc(s["pool_go"], 1)
                pool.indirect_dma_start(xg[:, u % 2, 0, :], None, xn_half,
                                        bass.IndirectOffsetOnAxis(ap=idx[:, u, 0:1], axis=0),
                                        bounds_check=2 * T - 1, oob_is_err=False).then_inc(gathered[u % 2], 16)
                with pool.If(full):
                    pool.indirect_dma_start(xg[:, u % 2, 1, :], None, xn_half,
                                            bass.IndirectOffsetOnAxis(ap=idx[:, u, 1:2], axis=0),
                                            bounds_check=2 * T - 1, oob_is_err=False).then_inc(gathered2[u % 2], 16)
                with pool.Else():
                    pool.dma_start(skipped[:, u:u + 1], halfc[0:1, :]).then_inc(gathered2[u % 2], 16)

            def scatter(r, i, u):
                e = r * NE + i * U + u
                full = is_full(r, i, u)
                pool.wait_ge(s["y0_evac"], e + 1)
                if not (isinstance(e, int) and e == 0):
                    pool.wait_ge(scattered[0], 16 * e)
                pool.sem_inc(s["pool_go"], 1)
                pool.indirect_dma_start(acc_rows[0], bass.IndirectOffsetOnAxis(ap=idx[:, u, 0:1], axis=0),
                                        yo[:, u % 2, 0, :], None, bounds_check=2 * T - 1, oob_is_err=False,
                                        compute_op=ALU.add).then_inc(scattered[0], 16)
                pool.wait_ge(s["y1_evac"], e + 1)
                if not (isinstance(e, int) and e == 0):
                    pool.wait_ge(scattered[1], 16 * e)
                pool.sem_inc(s["pool_go"], 1)
                with pool.If(full):
                    pool.indirect_dma_start(acc_rows[1], bass.IndirectOffsetOnAxis(ap=idx[:, u, 1:2], axis=0),
                                            yo[:, u % 2, 1, :], None, bounds_check=2 * T - 1, oob_is_err=False,
                                            compute_op=ALU.add).then_inc(scattered[1], 16)
                with pool.Else():
                    pool.dma_start(skipped[:, U + u:U + u + 1], halfc[0:1, :]).then_inc(scattered[1], 16)

            def body(r, i, first=False, last=False):
                for u in range(U):
                    if not (last and u >= U - 2):
                        gather(r, i + (u + 2) // U, (u + 2) % U)
                    if not (first and u == 0):
                        scatter(r, i if u else i - 1, (u - 1) % U)

            def rounds(r):
                gather(r, 0, 0)
                gather(r, 0, 1)
                body(r, 0, first=True)
                with pool.Fori(1, NE // U - 1) as i:
                    body(r, i)
                body(r, NE // U - 1, last=True)
                scatter(r, NE // U - 1, U - 1)
                for b in range(2):
                    pool.wait_ge(scattered[b], 16 * NE * (r + 1))

            pool.wait_ge(s["flags"], 1)
            rounds(0)
            most = pool.value_load(cnt_i[0:1, NE:NE + 1], min_val=0, max_val=T)
            for r in range(1, ROUNDS):
                with pool.If(most > r * ROUND):
                    rounds(r)
            pool.sem_inc(s["routed"], 1)
            ws = xn[0:64, 2, :]
            pool.wait_ge(acc_back[2], 32)
            pool.tensor_tensor(ws, ws, sh[0:64, 2, :], ALU.add).then_inc(s["fin_pool"], 1)
            pool.wait_ge(s["fin_pool"], 1)
            pool.tensor_tensor(ws, ws, gmod[0:64, 1, :], ALU.mult).then_inc(s["fin_pool"], 1)
            pool.wait_ge(s["fin_pool"], 2)
            pool.tensor_tensor(ws, ws, x[0:64, 2, :], ALU.add).then_inc(s["fin_pool"], 1)

        @block.scalar
        def _(act):
            nl = [0]

            def link(ins):
                nl[0] += 1
                ins.then_inc(act_link, 1)
                act.wait_ge(act_link, nl[0])

            def bc_evac_act():
                act.wait_ge(s["bc_ready"], 1)
                for g in range(4):
                    act.activation(mb_view(1, g), bc_view(g, 64), ACT.Copy).then_inc(s["bc_evac_a"], 1)
                act.wait_ge(s["bc_ready"], 2)
                for g in range(2):
                    act.activation(mb_view(0, g), bc_view(4 + g, P), ACT.Copy).then_inc(s["bc_evac_a"], 1)

            act.wait_ge(s["ld_c"], 32)
            act.activation(crow, crow, ACT.Silu).then_inc(s["csilu"], 1)
            act.wait_ge(s["ld_x"], 32)
            act.wait_ge(s["sumsq_v"], 2)
            for t, (t0, n) in enumerate(TILES):
                act.activation(xn[0:n, t, :], x[0:n, t, :], ACT.Square, accum_out=ssq[0:n, t:t + 1]).then_inc(s["sumsq"], 1)
            act.wait_ge(s["rs_in"], 4)
            act.activation(rstd, rstd, ACT.Sqrt).then_inc(s["rstd_ready"], 1)
            def xT_back(name, t):
                t0, n = TILES[t]
                for h in range(2):
                    act.wait_ge(s["tp_ready"], TP[f"{name}{t}{h}"] + 1)
                    act.activation(xT[:, 4 * h:4 * h + 4, t0:t0 + n],
                                   tp_bank(f"{name}{t}{h}")[:, :].rearrange("p (k n) -> p k n", k=4)[:, :, 0:n], ACT.Copy).then_inc(s["tp_evac"], 1)
            bc_evac_act()
            for t in range(3):
                xT_back("x", t)
            rows = [(0, io["state_conv"][0].rearrange("b j n -> (b j) n")), (24, io["state_lru_h"][0]), (32, io["conv_w"][0]),
                    (36, io["conv_b"]), (37, io["gate_r_b"]), (38, io["gate_i_b"]), (39, io["lru_lambda"]),
                    (40, io["out_norm_g"][:, 0:W])]
            for r0, src in rows:
                act.dma_start(chrow[r0:r0 + src.shape[0], :], src).then_inc(s["ld_ch"], 16)
            act.dma_start(wnat, io["sgu_w"][0].rearrange("g p q -> p g q")).then_inc(s["ld_sgu"], 16)
            act.wait_ge(s["blk_zero"], 3)
            for wt, name in ((wr, "gate_r_w"), (wi, "gate_i_w")):
                for h in range(2):
                    act.dma_start(wt[64 * h:64 * h + 64, :, 64 * h:64 * h + 64],
                                  io[name][0].rearrange("(c h) i j -> h i c j", h=2)[h]).then_inc(s["ld_rg"], 16)
            for b in range(NB):
                act.dma_start(wsn[8 * b:8 * b + 8, :, 8 * b:8 * b + 8],
                              io["sgu_w"][0, :, 0:NT, 0:NT].rearrange("g p q -> p g q")).then_inc(s["ld_wsn"], 16)
            act.dma_start(vg_row, io["sgu_norm_g"].to_broadcast([P, W])).then_inc(s["ld_rows"], 16)
            act.dma_start(og_row, io["out_norm_g"][:, W:2 * W].to_broadcast([P, W])).then_inc(s["ld_rows"], 16)
            act.dma_start(bsT, io["sgu_b"][0].rearrange("g p -> p g")).then_inc(s["ld_rows"], 16)
            for b in range(NB):
                act.dma_start(bsS[8 * b:8 * b + 8, :], io["sgu_b"][0, :, 0:NT].rearrange("g p -> p g")).then_inc(s["ld_rows"], 16)
            act.dma_start(wrt[:, :, :], io["router_w"][0].rearrange("(p k) e -> p k e", k=KT)).then_inc(s["ld_router"], 16)
            act.dma_start(rbias[:, :], io["router_bias"].to_broadcast([P, NE])).then_inc(s["ld_router"], 16)

            act.wait_ge(s["softp"], 2)
            act.activation(sp[1], sp[1], ACT.Exp, scale=-1.0).then_inc(s["softp_exp"], 1)

            act.wait_ge(s["x_pre"], 3)
            act.dma_start(gn[:, :], io["norm_ffn_g"].to_broadcast([P, D])).then_inc(s["gn_ffn"], 16)

            def prj(kind, n):
                act.wait_ge(s["prj_ready"], prj_no[(kind, n)] + 1)
                return prj_bank((kind, n))

            act.wait_ge(s["conv_step"], 1)
            for c in range(CT):
                b = prj("xa", c)
                link(act.activation(xap[:, c, CW - 1:SEG], b[:, 0:NPR], ACT.Copy))
                act.activation(xap[:, c, SEG:].rearrange("p (b j) -> p b j", b=NB)[:, :, CW - 1:],
                               b[:, NPR:T].rearrange("p (b j) -> p b j", b=NB), ACT.Copy).then_inc(s["prj_evac"], 1)
            for c in range(CT):
                act.activation(ga[:, c, :], prj("ga", c)[:, 0:T], ACT.Gelu_apprx_tanh).then_inc(s["prj_evac"], 1)
            act.wait_ge(s["acc_zeroed"], 32)
            for c in range(CT):
                act.activation(rr[:, c, :], prj("r", c)[:, 0:T], ACT.Sigmoid, bias=chT[:, c, 37:38]).then_inc(s["prj_evac"], 1)
            for c in range(CT):
                act.activation(ii[:, c, :], prj("i", c)[:, 0:T], ACT.Sigmoid, bias=chT[:, c, 38:39]).then_inc(s["prj_evac"], 1)
            for g in range(4):
                b = bc_view(4 + prj_no[("gm", g)] % 4, P)
                act.wait_ge(s["prj_ready"], prj_no[("gm", g)] + 1)
                act.activation(gmod_view(0, g), b[:, 0], ACT.Copy).then_inc(s["gm_in"], 1)
                act.activation(gmod_view(1, g), b[0:64, 1], ACT.Copy).then_inc(s["prj_evac"], 1)
            act.wait_ge(s["prj_evac"], prj_no[("i", CT - 1)] + 1)
            act.wait_ge(s["softp"], 15)
            for c in range(CT):
                act.activation(aa[:, c, :], rr[:, c, :], ACT.Exp, scale=s8[:, c:c + 1]).then_inc(s["expd"], 1)
            act.wait_ge(s["expd"], CT)
            for c in range(CT):
                act.activation(rr[:, c, :], rr[:, c, :], ACT.Tanh, scale=s8[:, c:c + 1]).then_inc(s["expd"], 1)
            act.wait_ge(s["lru_den"], 1)
            act.activation(rr, rr, ACT.Sqrt, scale=-1.0).then_inc(s["lru_sqrt"], 1)
            act.wait_ge(s["xn_free"], 1)

            def gelu(kind, dst):
                for t, (t0, n) in enumerate(TILES):
                    b = prj(kind, t)
                    if t < 2:
                        act.activation(dst[:, t, :], b[:, :], ACT.Gelu_apprx_tanh).then_inc(s["prj_evac"], 1)
                    else:
                        act.activation(dst[0:64, 2, 0:FE], b[0:64, 0:FE], ACT.Gelu_apprx_tanh).then_inc(s["gelu_half"], 1)
                        act.activation(dst[0:64, 2, FE:W], b[64:P, 0:FE], ACT.Gelu_apprx_tanh).then_inc(s["prj_evac"], 1)
            gelu("v", vv)
            act.wait_ge(s["gelu_half"], 1)
            for t, (t0, n) in enumerate(TILES):
                act.wait_ge(s["prj_evac"], prj_no[("v", t)] + 1)
                act.activation(us[0:n, t, :], vv[0:n, t, :], ACT.Square, accum_out=vss[0:n, t:t + 1]).then_inc(s["gv_sq"], 1)
            act.wait_ge(s["v_rs"], 4)
            act.activation(vrs, vrs, ACT.Sqrt).then_inc(s["v_sqrt"], 1)
            act.wait_ge(s["xn_done"], 2)
            act.wait_ge(s["xn_done_s"], 1)

            def ffn_back(w, kind):
                for g in range(4):
                    act.wait_ge(s["prj_ready"], prj_no[(kind, g)] + 1)
                    act.activation(mb_view(w, g), bc_view(4 + prj_no[(kind, g)] % 4, (P, 64)[w]), ACT.Copy).then_inc(s["prj_evac"], 1)
            ffn_back(0, "fp")
            act.wait_ge(s["gms_eps"], 5)
            act.activation(dd, dd, ACT.Sqrt).then_inc(s["gms_sqrt"], 1)
            act.wait_ge(s["gv_sq"], 3)
            gelu("u", us)
            ffn_back(1, "fs")
            for t, (t0, n) in enumerate(TILES):
                act.wait_ge(s["yb_step"], 7 * t + 6)
                act.activation(small[0:n, 16:24], small[0:n, 16:24], ACT.Sqrt).then_inc(s["yb_sqrt"], 1)
            for t, (t0, n) in enumerate(TILES):
                act.wait_ge(s["tp_ready"], TP[f"y{t}"] + 1)
                act.activation(xT[:, 4:8, t0:t0 + n], tp_bank(f"y{t}")[:, :].rearrange("p (k n) -> p k n", k=4)[:, :, 0:n],
                               ACT.Copy).then_inc(s["tp_evac"], 1)
            for t, (t0, n) in enumerate(TILES):
                if t == 2:
                    act.wait_ge(s["wout_ready"], 5)
                    act.activation(wo_hi, bank[WO_BANK[4]][64:P, :], ACT.Copy).then_inc(s["wo_moved"], 1)
                    xT_back("z", 1)
                act.wait_ge(s["x2_done"], t + 1)
                act.activation(sqy[0:n, :], x[0:n, t, :], ACT.Square, accum_out=ssq[0:n, t:t + 1]).then_inc(s["x2_sq"], 1)
                act.wait_ge(s["rs2_in"], 2 * t + 2)
                act.activation(rstd[0:n, t:t + 1], rstd[0:n, t:t + 1], ACT.Sqrt).then_inc(s["rs2"], 1)
                if t == 0:
                    xT_back("z", 0)

            def gf_back(g):
                b = bc_view(GF_BANK[g], P)
                act.wait_ge(s["gf_ready"], g + 1)
                act.activation(gmod_view(0, g), b[:, 0], ACT.Copy).then_inc(s["gf_in"], 1)
                act.activation(gmod_view(1, g), b[0:64, 1], ACT.Copy).then_inc(s["gf_in"], 1)
            xT_back("z", 2)
            gf_back(0)
            gf_back(1)
            act.activation(small[0:1, 59:60], rstd[0:1, 0:1], ACT.Sigmoid)
            act.wait_ge(s["pad_set"], 2)
            act.wait_ge(s["logit_done"], 3)
            for t, (t0, n) in enumerate(TILES):
                act.activation(score[0:n, t, :], bank[7][0:n, t * NE:(t + 1) * NE], ACT.Sigmoid).then_inc(s["sc_done"], 1)
            gf_back(2)
            gf_back(3)
            for t, (t0, n) in enumerate(TILES):
                act.wait_ge(s["sh_ready"], t + 1)
                if t == 2:
                    act.activation(up_s, bank[4 + t][64:P, 0:FE], ACT.Copy).then_inc(s["up_moved"], 1)
                if t:
                    act.wait_ge(s["sh_hid"], t)
                act.activation(sgs[0:n, :], bank[4 + t][0:n, 0:FE], ACT.Silu).then_inc(s["sh_act"], 1)

            def shared_out(t):
                n = TILES[t][1]
                for c in range(2):
                    act.wait_ge(s["sh_down_ready"], min(2 * t + c, 4) + 1)
                    b = bank[5 + c][:, :] if t < 2 else bank[5][64 * c:64 * c + 64, :]
                    act.activation(sh[0:n, t, c * HALF:(c + 1) * HALF], b, ACT.Copy).then_inc(s["sh_evac"], 1)

            act.wait_ge(s["out_small"], 64)
            shared_out(0)

            def xt1(r, i, u):
                act.wait_ge(s["xt_ready"], r * NE + i * U + u + 1)
                act.activation(xt[:, 1].rearrange("p k h n -> p (k h n)"), bank[3][:, :], ACT.Copy).then_inc(s["xt1_evac"], 1)

            def gates(r, i, u):
                e = r * NE + i * U + u
                act.wait_ge(s["gu_done"], e + 1)
                if not (isinstance(e, int) and e == 0):
                    act.wait_ge(s["hid_ready"], e)
                act.activation(sg[0:64, :], bank[u % 2][0:64, :], ACT.Silu).then_inc(s["sg_evac"], 1)
                act.activation(up[0:64, :], bank[u % 2][64:P, :], ACT.Copy).then_inc(s["up_evac"], 1)

            def y1(r, i, u):
                e = r * NE + i * U + u
                act.wait_ge(s["y_ready"], e + 1)
                act.wait_ge(s["idx_ready"], e + 1)
                if not (isinstance(e, int) and e < 2):
                    act.wait_ge(scattered[1], 16 * e - 16)
                act.activation(yo[:, u % 2, 1, :], bank[6][:, :], ACT.Copy, scale=pick_out[:, u, 1, 1:2]).then_inc(s["y1_evac"], 1)

            def body(r, i, first=False, last=False):
                for u in range(U):
                    gates(r, i, u)
                    if not (last and u == U - 1):
                        xt1(r, i + (u + 1) // U, (u + 1) % U)
                    if first and u == 0 and r == 0:
                        shared_out(1)
                        shared_out(2)
                    if not (first and u == 0):
                        y1(r, i if u else i - 1, (u - 1) % U)

            def rounds(r):
                xt1(r, 0, 0)
                body(r, 0, first=True)
                with act.Fori(1, NE // U - 1) as i:
                    body(r, i)
                body(r, NE // U - 1, last=True)
                y1(r, NE // U - 1, U - 1)

            rounds(0)
            most = act.value_load(cnt_i[0:1, NE:NE + 1], min_val=0, max_val=T)
            for r in range(1, ROUNDS):
                with act.If(most > r * ROUND):
                    rounds(r)
            act.dma_start(gn[:, :], io["final_norm_g"].rearrange("(o n) -> o n", o=1).to_broadcast([P, D])).then_inc(s["gn_fin"], 16)
            for t in FIN_ORDER:
                n = TILES[t][1]
                if t == 2:
                    act.wait_ge(s["fin_pool"], 3)
                else:
                    act.wait_ge(s["fin_sq"], 3 * t + 3)
                act.activation(sqy[0:n, :], xn[0:n, t, :], ACT.Square, accum_out=fss[0:n, t:t + 1]).then_inc(s["fin_rs"], 1)
                act.wait_ge(s["rs_in"], 4 + 2 * FIN_ORDER.index(t) + 2)
                act.activation(frs[0:n, t:t + 1], frs[0:n, t:t + 1], ACT.Sqrt).then_inc(s["fin_rs"], 1)

        @block.tensor
        def _(pe):
            def tp_wait(n):
                if TP[n] >= 2:
                    pe.wait_ge(s["tp_evac"], TP[n] - 1)
                return tp_bank(n)

            def piece(kind, j):
                n = piece_no[(kind, j)]
                pe.wait_ge(ld_piece[n % SLOTS], 16 * (n // SLOTS + 1))
                return gu[n % SLOTS]

            def ada(j):
                w = piece("ada", j)
                if j >= 2:
                    pe.wait_ge(s["mod_evac"], j - 1)
                for k in range(KT):
                    for g in range(4):
                        mm = pe.matmul(bank[j % 2][32 * g:32 * g + 32, 0:P], cT[:, k, :], w[:, k, g * P:(g + 1) * P],
                                       start=(k == 0), stop=(k == KT - 1))
                mm.then_inc(s["mod_ready"], 1)

            def prj_wait(kind, n):
                no = prj_no[(kind, n)]
                if no >= 4:
                    pe.wait_ge(s["prj_evac"], no - 3)
                return prj_bank((kind, n))

            def channels(kind, j):
                w = piece("in", j)
                for c in range(CT):
                    b = prj_wait(kind, c)
                    for k in range(KT):
                        mm = pe.matmul(b[:, 0:T], w[:, k, c * P:(c + 1) * P], xT[:, k, :], start=(k == 0), stop=(k == KT - 1))
                    mm.then_inc(s["prj_ready"], 1)

            def tile_product(b, t, w, width, ks=range(KT)):
                t0, n = TILES[t]
                for k in ks:
                    if t < 2:
                        mm = pe.matmul(b[:, 0:width], xT[:, k, t0:t0 + n], w[:, k, :], start=(k == 0), stop=(k == KT - 1))
                    else:
                        for c in range(2):
                            mm = pe.matmul(b[64 * c:64 * c + 64, 0:width // 2], xT[:, k, t0:t0 + n],
                                           w[:, k, c * width // 2:(c + 1) * width // 2], start=(k == 0), stop=(k == KT - 1))
                return mm

            def tokens(kind, j):
                w = piece("in", j)
                for t in range(3):
                    tile_product(prj_wait(kind, t), t, w, W).then_inc(s["prj_ready"], 1)

            def spread(b, w, g, j0, j1, col=0):
                if w == 0:
                    rows = ident[:, 32 * g:32 * g + 1].to_broadcast([P, P])
                else:
                    rows = spread_s[:, g, :]
                return pe.matmul(bank[b][0:(P, 64)[w], col:col + (j1 - j0) * P], rows, mods[:, j0:j1, :], start=True, stop=True)

            pe.wait_ge(s["consts"], 6)
            pe.wait_ge(s["csilu"], 1)
            pe.wait_ge(s["consts_v"], 5)
            b = tp_wait("c")
            for k in range(KT):
                mm = pe.transpose(b[:, 32 * k:32 * k + NSEQ], crow[:, k::KT], ident[0:NSEQ, 0:NSEQ])
            mm.then_inc(s["tp_ready"], 1)
            pe.wait_ge(s["tp_evac"], 1)
            def keep_warm(n, b=4):
                for _ in range(n):
                    pe.matmul(bank[b][:, 0:P], ones[:, :], ident[:, :], start=True, stop=True)

            for j in range(4):
                ada(j)
                if j == 2:
                    keep_warm(20)
            def turn(name, done, t):
                t0, n = TILES[t]
                if done == "xn_done" and t == 2:
                    pe.wait_ge(s["xn_done_s"], 1)
                else:
                    pe.wait_ge(s[done], t + 1)
                for h in range(2):
                    b = tp_wait(f"{name}{t}{h}")
                    for k in range(4):
                        mm = pe.transpose(b[:, k * P:k * P + n], xn[0:n, t, (4 * h + k) * P:(4 * h + k + 1) * P], ident[0:n, 0:n])
                    mm.then_inc(s["tp_ready"], 1)

            pe.wait_ge(s["spread_in"], 1)
            pe.wait_ge(s["mod_evac"], 4)
            for w in (1, 0):
                for g in range(4):
                    mm = spread(g if w else 4 + g, w, g, 0, 4)
                mm.then_inc(s["bc_ready"], 1)
            pe.wait_ge(s["bc_evac_a"], 4)
            keep_warm(20, 0)
            for t in range(3):
                turn("x", "xn_done", t)
            pe.wait_ge(s["tp_evac"], TP["x21"] + 1)
            channels("xa", 0)
            pe.wait_ge(s["ld_ch"], 16 * 8)
            b = tp_wait("ch")
            for c in range(CT):
                mm = pe.transpose(b[:, 41 * c:41 * c + 41], chrow[0:41, c * P:(c + 1) * P], ident[0:41, 0:41])
            mm.then_inc(s["tp_ready"], 1)
            ada(4)
            ada(5)
            channels("ga", 1)
            ada(6)
            pe.wait_ge(s["ld_rg"], 64)
            pe.wait_ge(s["conv_done"], 1)
            for kind, wt in (("r", wr), ("i", wi)):
                if kind == "i":
                    ada(7)
                for c in range(CT):
                    pe.matmul(prj_wait(kind, c)[:, 0:T], wt[:, c, :], xc[:, c, :], start=True, stop=True).then_inc(s["prj_ready"], 1)
            pe.wait_ge(s["msk"], 2)
            for h in range(2):
                b = tp_wait(f"w{h}")
                for g in range(4):
                    mm = pe.transpose(b[:, g * P:(g + 1) * P], wnat[:, 4 * h + g, :], ident[:, :])
                mm.then_inc(s["tp_ready"], 1)
            b = tp_wait("ws")
            for g in range(8):
                mm = pe.transpose(b[0:64, g * 64:(g + 1) * 64], wsn[0:64, g, :], ident[0:64, 0:64])
            mm.then_inc(s["tp_ready"], 1)
            pe.wait_ge(s["mod_evac"], 6)
            for g in range(4):
                b = 4 + prj_no[("gm", g)] % 4
                prj_wait("gm", g)
                spread(b, 0, g, 4, 6)
                spread(b, 1, g, 4, 6, FE).then_inc(s["prj_ready"], 1)
            tokens("v", 3)
            ada(8)
            ada(9)
            pe.wait_ge(s["ya_sq"], 2)
            for c in range(CT):
                pe.matmul(tp_wait(f"g{c}")[:, 0:T], blk[:, :], dd[:, c, :], start=True, stop=True).then_inc(s["tp_ready"], 1)
            def spread_ffn(w, kind):
                for g in range(4):
                    prj_wait(kind, g)
                    spread(4 + prj_no[(kind, g)] % 4, w, g, 6, 10).then_inc(s["prj_ready"], 1)
            pe.wait_ge(s["mod_evac"], 10)
            spread_ffn(0, "fp")
            tokens("u", 2)
            ada(10)
            ada(11)
            spread_ffn(1, "fs")
            pe.wait_ge(s["v_done"], 3)
            for t, (t0, n) in enumerate(TILES):
                b = tp_wait(f"s{t}")
                for g in range(8):
                    w = wT[:, g, :] if t < 2 else wsT[0:64, g, :]
                    mm = pe.matmul(b[0:n, g * 64:(g + 1) * 64], w, vv[0:n, t, g * 64:(g + 1) * 64], start=True, stop=True)
                mm.then_inc(s["tp_ready"], 1)
            w = [piece("out", 0), piece("out", 1)]
            pe.wait_ge(s["prj_evac"], len(PRJ))
            pe.wait_ge(s["mod_evac"], 12)
            pe.wait_ge(s["ya_done"], CT)

            def wout(t, ks):
                t0, n = TILES[t]
                for c in range(2):
                    b = bank[WO_BANK[2 * t + c]] if t < 2 else bank[WO_BANK[4]]
                    if t < 2:
                        for k in ks:
                            mm = pe.matmul(b[:, :], xT[:, k, t0:t0 + n], w[c][:, k, :], start=(k == 0), stop=(k == KT - 1))
                        if ks[-1] == KT - 1:
                            mm.then_inc(s["wout_ready"], 1)
                if t == 2:
                    for k in ks:
                        for c in range(2):
                            mm = pe.matmul(b[64 * c:64 * c + 64, :], xT[:, k, t0:t0 + n], w[c][:, k, :], start=(k == 0), stop=(k == KT - 1))
                    if ks[-1] == KT - 1:
                        mm.then_inc(s["wout_ready"], 1)
            for t in range(3):
                wout(t, range(4))
            pe.wait_ge(s["lru_h"], 2)

            def turn_y(t):
                n = TILES[t][1]
                pe.wait_ge(s["yb_step"], 7 * t + 7)
                b = tp_wait(f"y{t}")
                for k in range(4):
                    mm = pe.transpose(b[:, k * P:k * P + n], us[0:n, t, k * P:(k + 1) * P], ident[0:n, 0:n])
                mm.then_inc(s["tp_ready"], 1)
            pe.wait_ge(s["tp_evac"], TP["s2"] + 1)
            turn_y(0)
            turn_y(1)
            pe.wait_ge(s["tp_evac"], TP["y0"] + 1)
            wout(0, range(4, KT))
            turn_y(2)
            pe.wait_ge(s["tp_evac"], TP["y2"] + 1)
            b = tp_wait("hc")
            for c in range(CT):
                mm = pe.transpose(b[0:36, c * P:(c + 1) * P], hc[:, c, :], ident[:, :])
            mm.then_inc(s["tp_ready"], 1)
            wout(1, range(4, KT))
            wout(2, range(4, KT))
            def shared_gu(t):
                tile_product(bank[4 + t], t, gu[SH_SLOT], 2 * FE).then_inc(s["sh_ready"], 1)

            def logits(t):
                t0, n = TILES[t]
                for k in range(KT):
                    mm = pe.matmul(bank[7][0:n, t * NE:(t + 1) * NE], xT[:, k, t0:t0 + n], wrt[:, k, :], start=(k == 0), stop=(k == KT - 1))
                mm.then_inc(s["logit_done"], 1)
            def spread_gf(g):
                spread(GF_BANK[g], 0, g, 10, 12)
                spread(GF_BANK[g], 1, g, 10, 12, FE).then_inc(s["gf_ready"], 1)

            turn("z", "xn_ready", 0)
            pe.wait_ge(s["tp_evac"], TP["z01"] + 1)
            pe.wait_ge(s["ld_router"], 32)
            logits(0)
            pe.wait_ge(ld_shared_gu, 32)
            tile_product(bank[4], 0, gu[SH_SLOT], 2 * FE, range(4))
            turn("z", "xn_ready", 1)
            tile_product(bank[4], 0, gu[SH_SLOT], 2 * FE, range(4, KT)).then_inc(s["sh_ready"], 1)
            pe.wait_ge(s["tp_evac"], TP["z11"] + 1)
            logits(1)
            turn("z", "xn_ready", 2)
            pe.wait_ge(s["x2_done"], 3)
            pe.wait_ge(s["mod_evac"], 12)
            for c in range(2, 4):
                pe.matmul(bank[1][:, c * P:(c + 1) * P], ident[:, :], ident[:, :], start=True, stop=True)
            spread_gf(0)
            spread_gf(1)
            pe.wait_ge(s["tp_evac"], TP["z21"] + 1)
            logits(2)
            spread_gf(2)
            pe.wait_ge(s["gf_in"], 2)
            spread_gf(3)
            tile_product(bank[5], 1, gu[SH_SLOT], 2 * FE, range(4))
            pe.wait_ge(s["mask_done"], 1)
            b = tp_wait("pos")
            for t, (t0, n) in enumerate(TILES):
                for q in range(t + 1):
                    m = TILES[q][1]
                    mm = pe.matmul(b[0:n, t * NE:(t + 1) * NE], (upper if q == t else ones)[0:m, 0:n], mask[0:m, q, :],
                                   start=(q == 0), stop=(q == t))
            for q in range(3):
                m = TILES[q][1]
                mm = pe.matmul(b[:, 3 * NE:4 * NE], ones[0:m, :], mask[0:m, q, :], start=(q == 0), stop=(q == 2))
            mm.then_inc(s["tp_ready"], 1)
            tile_product(bank[5], 1, gu[SH_SLOT], 2 * FE, range(4, KT)).then_inc(s["sh_ready"], 1)

            def pick(r, i, u):
                e = r * NE + i * U + u
                pe.wait_ge(s["sel_built"], e + 1)
                if isinstance(e, int) and e == 0:
                    pe.wait_ge(s["sc_done"], 3)
                else:
                    pe.wait_ge(s["gate_ready"], e)
                for b in range(2):
                    for t, (t0, n) in enumerate(TILES):
                        mm = pe.matmul(bank[7][:, 6 * b:6 * b + 6], sel[0:n, t, b * P:(b + 1) * P],
                                       tg[0:n, t, bass.ds(i * U + u, 1)].rearrange("p e c m -> p (e c m)"),
                                       start=(t == 0), stop=(t == 2))
                mm.then_inc(s["sel_ready"], 1)

            def turn_x(r, i, u, full):
                e = r * NE + i * U + u
                pe.wait_ge(gathered[u % 2], 8 * (e - u % 2) + 16)
                pe.wait_ge(gathered2[u % 2], 8 * (e - u % 2) + 16)
                if isinstance(e, int) and e == 0:
                    pe.wait_ge(s["sc_done"], 3)
                    pe.wait_ge(s["tp_evac"], len(TP))
                else:
                    pe.wait_ge(s["xt0_evac"], e)
                    pe.wait_ge(s["xt1_evac"], e)

                def half(b):
                    for k in range(4):
                        pe.transpose(bank[2 + b][:, k * P:(k + 1) * P], xg[:, u % 2, b, k * P:(k + 1) * P], ident[:, :])
                with pe.If(full):
                    half(1)
                for k in range(4):
                    mm = pe.transpose(bank[2][:, k * P:(k + 1) * P], xg[:, u % 2, 0, k * P:(k + 1) * P], ident[:, :])
                mm.then_inc(s["xt_ready"], 1)

            def gate_up(r, i, u, full):
                e = r * NE + i * U + u
                pe.wait_ge(ld_gu[gslot(u)], 8 * (e - u % SLOTS) + 32)
                pe.wait_ge(s["xt0_evac"], e + 1)
                pe.wait_ge(s["xt1_evac"], e + 1)
                if isinstance(e, int) and e < 2:
                    pe.wait_ge(s["gf_in"], 8)
                else:
                    pe.wait_ge(s["up_evac"], e - 1)
                w = gu[gslot(u)]

                def blocks(b):
                    for k in range(KT):
                        for c in range(2):
                            mm = pe.matmul(bank[u % 2][64 * c:64 * c + 64, b * FE:(b + 1) * FE], xt[:, b, k % 4, k // 4, :],
                                           w[:, k, c * FE:(c + 1) * FE], start=(k == 0), stop=(k == KT - 1))
                    return mm
                with pe.If(full):
                    blocks(1)
                blocks(0).then_inc(s["gu_done"], 1)

            def turn_h(r, i, u, full):
                e = r * NE + i * U + u
                pe.wait_ge(s["hid_ready"], e + 1)
                if isinstance(e, int) and e == 0:
                    pe.wait_ge(s["h_evac"], 3)
                else:
                    pe.wait_ge(s["ht_evac"], e)

                def half(b):
                    for j in range(2):
                        mm = pe.transpose(bank[4][:, (2 * b + j) * 64:(2 * b + j + 1) * 64], hid[0:64, b, j, :], ident[0:64, 0:64])
                    return mm
                with pe.If(full):
                    half(1)
                half(0).then_inc(s["ht_ready"], 1)

            def down(r, i, u, full):
                e = r * NE + i * U + u
                pe.wait_ge(ld_dn[dslot(u)], 4 * (e - u % SLOTS) + 16)
                pe.wait_ge(s["ht_evac"], e + 1)
                if isinstance(e, int) and e == 0:
                    pe.wait_ge(s["sh_evac"], 6)
                else:
                    pe.wait_ge(s["y0_evac"], e)
                    pe.wait_ge(s["y1_evac"], e)

                def blocks(b):
                    for j in range(2):
                        for c in range(2):
                            mm = pe.matmul(bank[5 + b][64 * c:64 * c + 64, :], hT[:, b, j, :],
                                           dn[:, dslot(u), j * D + c * HALF:j * D + (c + 1) * HALF], start=(j == 0), stop=(j == 1))
                    return mm
                with pe.If(full):
                    blocks(1)
                blocks(0).then_inc(s["y_ready"], 1)

            def is_full(r, i, u):
                return pe.value_load(cnt_i[0:1, bass.ds(i * U + u, 1)], min_val=0, max_val=T) > (r * ROUND + 64)

            def body(r, i, first=False, last=False):
                now = is_full(r, i, 0)
                before = None if first else is_full(r, i - 1, U - 1)
                for u in range(U):
                    gate_up(r, i, u, now)
                    if first and u == 1 and r == 0:
                        shared_down(1)
                        shared_down(2)
                    if before is not None:
                        turn_h(r, i if u else i - 1, (u - 1) % U, before)
                    if not (last and u >= U - 2):
                        pick(r, i + (u + 2) // U, (u + 2) % U)
                    after = None
                    if not (last and u == U - 1):
                        after = is_full(r, i + (u + 1) // U, (u + 1) % U)
                        turn_x(r, i + (u + 1) // U, (u + 1) % U, after)
                    if before is not None:
                        down(r, i if u else i - 1, (u - 1) % U, before)
                    before, now = now, after
                return before

            def shared_down(t):
                t0, n = TILES[t]
                pe.wait_ge(s["sh_hid"], t + 1)
                if t:
                    pe.wait_ge(s["h_evac"], t)
                for j in range(2):
                    mm = pe.transpose(bank[4][:, j * P:j * P + n], shid[0:n, j * P:(j + 1) * P], ident[0:n, 0:n])
                mm.then_inc(s["h_ready"], 1)
                if t == 0:
                    pe.wait_ge(ld_shared_dn, 16)
                    pe.wait_ge(s["sh_hid"], 2)
                    pe.wait_ge(s["sh_act"], 3)
                else:
                    pe.wait_ge(s["sh_evac"], 2 * t)
                pe.wait_ge(s["h_evac"], t + 1)

                def product(c, j):
                    dst = bank[5 + c][:, :] if t < 2 else bank[5][64 * c:64 * c + 64, :]
                    return pe.matmul(dst, shT[:, j, 0:n], dn[:, 0, j * D + c * HALF:j * D + (c + 1) * HALF],
                                     start=(j == 0), stop=(j == 1))
                if t < 2:
                    for c in range(2):
                        product(c, 0)
                        product(c, 1).then_inc(s["sh_down_ready"], 1)
                else:
                    for j in range(2):
                        product(0, j)
                        mm = product(1, j)
                    mm.then_inc(s["sh_down_ready"], 1)

            def rounds(r):
                pick(r, 0, 0)
                if r == 0:
                    pe.wait_ge(s["flags"], 1)
                    pe.wait_ge(s["gf_in"], 6)
                    shared_gu(2)
                pick(r, 0, 1)
                if r == 0:
                    shared_down(0)
                turn_x(r, 0, 0, is_full(r, 0, 0))
                body(r, 0, first=True)
                with pe.Fori(1, NE // U - 1) as i:
                    body(r, i)
                before = body(r, NE // U - 1, last=True)
                turn_h(r, NE // U - 1, U - 1, before)
                down(r, NE // U - 1, U - 1, before)

            rounds(0)
            most = pe.value_load(cnt_i[0:1, NE:NE + 1], min_val=0, max_val=T)
            for r in range(1, ROUNDS):
                with pe.If(most > r * ROUND):
                    rounds(r)

        @block.vector
        def _(dve):
            nl = [0]

            def link(ins):
                nl[0] += 1
                ins.then_inc(dve_link, 1)
                dve.wait_ge(dve_link, nl[0])

            def tp_get(n):
                dve.wait_ge(s["tp_ready"], TP[n] + 1)
                return tp_bank(n)

            dve.memset(cT[:, :, :], 0.0).then_inc(s["cT_zero"], 1)
            dve.memset(adab, 0.0).then_inc(s["adab_zero"], 1)
            dve.memset(wr, 0.0).then_inc(s["blk_zero"], 1)
            dve.memset(wi, 0.0).then_inc(s["blk_zero"], 1)
            dve.memset(wsn[0:64], 0.0).then_inc(s["blk_zero"], 1)
            dve.memset(xap[:, :, 0:CW - 1], 0.0).then_inc(s["conv_step"], 1)
            dve.memset(ssq, 1.0).then_inc(s["sumsq_v"], 1)
            dve.memset(vss, 1.0).then_inc(s["sumsq_v"], 1)
            dve.memset(halfc[0:64, :], float(OOB)).then_inc(s["consts_v"], 1)
            dve.memset(halfc[64:P, :], float(OOB + 1)).then_inc(s["consts_v"], 1)
            dve.memset(blk[:, :], 0.0).then_inc(s["consts_v"], 1)
            dve.wait_ge(s["consts_v"], 3)
            dve.memset(blk[0:64, 0:64], 1.0 / 64).then_inc(s["consts_v"], 1)
            dve.memset(blk[64:P, 64:P], 1.0 / 64).then_inc(s["consts_v"], 1)
            dve.wait_ge(s["cT_zero"], 1)
            dve.wait_ge(s["consts"], 6)
            dve.tensor_copy(spread_s.rearrange("p g (b t) -> p g b t", b=NB),
                            ident[:, :].rearrange("p (g r o) -> p g r o", g=4, o=1)[:, :, 1:NSEQ, :].to_broadcast([P, 4, NB, NT]))               .then_inc(s["spread_in"], 1)
            dve.tensor_copy(cT[:, :, 0:NSEQ], tp_get("c")[:, 0:256].rearrange("p (k c) -> p k c", k=KT)[:, :, 0:NSEQ]).then_inc(s["tp_evac"], 1)
            dve.memset(dnf[:, 0:2560], 0.0).then_inc(s["zero_ready"], 1)
            dve.wait_ge(s["sumsq_v"], 2)
            dve.wait_ge(s["sumsq"], 3)
            for t, (t0, n) in enumerate(TILES):
                dve.tensor_scalar(rstd[0:n, t:t + 1], ssq[0:n, t:t + 1], 1.0 / D, EPS, ALU.mult, ALU.add).then_inc(s["rs_in"], 1)
            dve.wait_ge(s["rs_in"], 3)
            dve.memset(rstd[64:P, 2:3], 1.0).then_inc(dve_link, 1)
            nl[0] += 1
            dve.wait_ge(dve_link, nl[0])
            dve.reciprocal(rstd, rstd).then_inc(s["rs_in"], 1)
            def mod(j):
                dve.wait_ge(s["mod_ready"], j + 1)
                dve.tensor_tensor(mods[:, j, :], bank[j % 2][:, 0:P], adab[:, j, :], ALU.add).then_inc(s["mod_evac"], 1)
            dve.wait_ge(s["ld_adab"], 64)
            for j in range(3):
                mod(j)
            work = dnf[:, 2560:2560 + 2 * D]
            dve.wait_ge(s["rstd_ready"], 1)
            dve.wait_ge(s["ld_gn"], 16)
            for t, (t0, n) in enumerate(TILES):
                dst = work[:, t * D:(t + 1) * D] if t < 2 else xs_pre
                dve.scalar_tensor_tensor(dst, x[0:n, t, :], rstd[0:n, t:t + 1], gn[0:n, :], ALU.mult, ALU.mult).then_inc(s["x_pre"], 1)
            mod(3)
            def scales(sm_gn, gn_count):
                dve.wait_ge(s[sm_gn], gn_count)
                dve.scalar_tensor_tensor(mb[:, 1, 0, :], mb[:, 1, 0, :], 1.0, gn[:, :], ALU.add, ALU.mult).then_inc(s["mod_scaled"], 1)
                dve.scalar_tensor_tensor(mb[0:64, 1, 1, :], mb[0:64, 1, 1, :], 1.0, gn[0:64, :], ALU.add, ALU.mult).then_inc(s["mod_scaled"], 1)

            def normed(t, done, work):
                n = TILES[t][1]
                w = t // 2
                link(dve.scalar_tensor_tensor(work[0:n, :], x[0:n, t, :], rstd[0:n, t:t + 1], mb[0:n, 1, w, :], ALU.mult, ALU.mult))
                dve.tensor_tensor(xn[0:n, t, :].rearrange("t (k p) -> t p k", k=KT), work[0:n, :].rearrange("t (p k) -> t p k", k=KT),
                                  mb[0:n, 0, w, :].rearrange("t (p k) -> t p k", k=KT), ALU.add).then_inc(s[done], 1)

            dve.wait_ge(s["bc_ready"], 2)
            for g in range(2, 4):
                dve.tensor_copy(mb_view(0, g), bc_view(4 + g, P)).then_inc(s["bc_evac_v"], 1)
            dve.wait_ge(s["bc_evac_v"], 2)
            dve.wait_ge(s["bc_evac_a"], 6)
            for t in range(2):
                w = work[:, t * D:(t + 1) * D]
                link(dve.scalar_tensor_tensor(w, mb[:, 1, 0, :], 1.0, w, ALU.add, ALU.mult))
                dve.tensor_tensor(xn[:, t, :].rearrange("t (k p) -> t p k", k=KT), w.rearrange("t (p k) -> t p k", k=KT),
                                  mb[:, 0, 0, :].rearrange("t (p k) -> t p k", k=KT), ALU.add).then_inc(s["xn_done"], 1)

            dve.wait_ge(s["tp_evac"], TP["x21"] + 1)
            dve.memset(spare, 0.0).then_inc(s["xn_free"], 1)
            dve.tensor_copy(chT[:, :, :], tp_get("ch")[:, 0:41 * CT].rearrange("p (c r) -> p c r", c=CT)).then_inc(s["tp_evac"], 1)
            sf = [0]

            def soft(ins):
                sf[0] += 1
                ins.then_inc(s["softp"], 1)
                dve.wait_ge(s["softp"], sf[0])
            dve.wait_ge(s["tp_evac"], TP["ch"] + 1)
            soft(dve.tensor_scalar(sp[0], lam, -1.0, None, ALU.mult))
            soft(dve.tensor_tensor(sp[1], lam, sp[0], ALU.max))
            dve.wait_ge(s["softp_exp"], 1)
            soft(dve.tensor_scalar(sp[2], sp[1], 2.0, None, ALU.add))
            soft(dve.reciprocal(sp[2], sp[2]))
            soft(dve.tensor_tensor(sp[3], sp[1], sp[2], ALU.mult))
            soft(dve.tensor_tensor(sp[4], sp[3], sp[3], ALU.mult))
            soft(dve.tensor_scalar(sp[5], sp[4], 1.0 / 15, None, ALU.mult))
            for m in (13, 11, 9, 7, 5):
                soft(dve.scalar_tensor_tensor(sp[5], sp[5], 1.0 / m, sp[4], ALU.add, ALU.mult))
            link(dve.scalar_tensor_tensor(sp[5], sp[5], 1.0 / 3, sp[4], ALU.add, ALU.mult))
            link(dve.scalar_tensor_tensor(sp[5], sp[5], 1.0, sp[3], ALU.add, ALU.mult))
            soft(dve.tensor_scalar(sp[0], sp[0], 0.0, -8.0, ALU.max, ALU.mult))
            soft(dve.tensor_scalar(sp[5], sp[5], -16.0, None, ALU.mult))
            soft(dve.tensor_tensor(s8, sp[5], sp[0], ALU.add))
            dve.tensor_copy(xap[:, :, SEG:].rearrange("p c (b j) -> p c b j", b=NB)[:, :, :, 0:CW - 1],
                            chT[:, :, 0:24].rearrange("p c (b j) -> p c b j", b=NB)).then_inc(s["conv_step"], 1)

            dve.wait_ge(s["acc_zeroed"], 32)
            dve.wait_ge(s["conv_step"], 2)
            dve.wait_ge(s["prj_evac"], CT)
            xas = xap[:, :, SEG:].rearrange("p c (b j) -> p c b j", b=NB)
            xcs = xc[:, :, NPR:].rearrange("p c (b j) -> p c b j", b=NB)
            for k in range(CW):
                for c in range(CT):
                    for dst, src in ((xc[:, c, 0:NPR], xap[:, c, k:k + NPR]), (xcs[:, c], xas[:, c, :, k:k + NT])):
                        wk = chT[:, c, 32 + k:33 + k]
                        if k == 0:
                            ins = dve.tensor_scalar(dst, src, wk, chT[:, c, 36:37], ALU.mult, ALU.add)
                        else:
                            ins = dve.scalar_tensor_tensor(dst, src, wk, dst, ALU.mult, ALU.add)
                        ins.then_inc(s["conv_step"], 1)
                dve.wait_ge(s["conv_step"], 2 + 2 * CT * (k + 1))
            link(dve.tensor_copy(hc[:, :, 9:12], xap[:, :, SEG - 3:SEG]))
            dve.tensor_copy(hc[:, :, 12:36].rearrange("p c (b j) -> p c b j", b=NB), xas[:, :, :, NT:SS]).then_inc(s["conv_done"], 1)
            mod(4)
            mod(5)
            for h in range(2):
                dve.tensor_copy(wT[:, 4 * h:4 * h + 4, :], tp_get(f"w{h}")[:, :].rearrange("p (g q) -> p g q", g=4)).then_inc(s["tp_evac"], 1)
            dve.tensor_copy(wsT[0:64], tp_get("ws")[0:64, :].rearrange("p (g q) -> p g q", g=8)).then_inc(s["tp_evac"], 1)

            dve.wait_ge(s["expd"], CT)
            dve.tensor_tensor(dd, aa, aa, ALU.mult).then_inc(s["lru_asq"], 1)
            dve.wait_ge(s["expd"], 2 * CT)
            link(dve.tensor_tensor(ii, ii, xc, ALU.mult))
            dve.wait_ge(s["lru_asq"], 1)
            dve.scalar_tensor_tensor(rr, dd, 1.0, rr, ALU.add, ALU.mult).then_inc(s["lru_den"], 1)
            mod(6)
            mod(7)
            dve.wait_ge(s["lru_sqrt"], 1)
            link(dve.tensor_tensor(ii, ii, rr, ALU.mult))
            a0 = aa[:, :, NPR:].rearrange("p c (b j) -> p c b j", b=NB)[:, :, :, 0]
            u0 = ii[:, :, NPR:].rearrange("p c (b j) -> p c b j", b=NB)[:, :, :, 0]
            h0 = dd[:, :, 0:NB]
            link(dve.tensor_tensor(h0, a0, chT[:, :, 24:32], ALU.mult))
            link(dve.tensor_tensor(u0, u0, h0, ALU.add))
            link(dve.memset(a0, 0.0))
            link(dve.memset(aa[:, :, 0:1], 0.0))
            link(dve.tensor_tensor_scan(xc.rearrange("p c t -> p (c t)"), aa.rearrange("p c t -> p (c t)"),
                                        ii.rearrange("p c t -> p (c t)"), 0.0, ALU.mult, ALU.add))
            dve.tensor_copy(hc[:, :, 0:1], xc[:, :, NPR - 1:NPR]).then_inc(s["lru_h"], 1)
            dve.tensor_copy(hc[:, :, 1:9], xc[:, :, NPR:].rearrange("p c (b j) -> p c b j", b=NB)[:, :, :, NT - 1]).then_inc(s["lru_h"], 1)
            dve.wait_ge(s["prj_evac"], 2 * CT)
            dve.tensor_tensor(ga, ga, xc, ALU.mult).then_inc(s["ya_sq"], 1)
            dve.wait_ge(s["ya_sq"], 1)
            dve.tensor_tensor(dd, ga, ga, ALU.mult).then_inc(s["ya_sq"], 1)
            mod(8)
            mod(9)
            dve.wait_ge(s["gv_sq"], 3)
            for t, (t0, n) in enumerate(TILES):
                dve.tensor_scalar(vrs[0:n, t:t + 1], vss[0:n, t:t + 1], 1.0 / W, EPS, ALU.mult, ALU.add).then_inc(s["v_rs"], 1)
            dve.wait_ge(s["v_rs"], 3)
            link(dve.memset(vrs[64:P, 2:3], 1.0))
            dve.reciprocal(vrs, vrs).then_inc(s["v_rs"], 1)
            for c in range(CT):
                dve.tensor_scalar(dd[:, c, :], tp_get(f"g{c}")[:, 0:T], EPS, None, ALU.add).then_inc(s["tp_evac"], 1)
            dve.wait_ge(s["v_sqrt"], 1)
            dve.wait_ge(s["ld_rows"], 16 * 11)
            for t, (t0, n) in enumerate(TILES):
                dve.scalar_tensor_tensor(vv[0:n, t, :], vv[0:n, t, :], vrs[0:n, t:t + 1], vg_row[0:n, :], ALU.mult, ALU.mult).then_inc(s["v_done"], 1)
            dve.wait_ge(s["tp_evac"], TP[f"g{CT - 1}"] + 1)
            for c in range(4):
                dve.reciprocal(dd[:, c, :], dd[:, c, :]).then_inc(s["gms_eps"], 1)
            dve.memset(spare, 0.0).then_inc(s["gms_eps"], 1)
            dve.wait_ge(s["gms_sqrt"], 1)
            link(dve.tensor_tensor(ga, ga, dd, ALU.mult))
            mod(10)
            mod(11)
            for c in range(CT):
                dve.tensor_scalar(xT[:, c, :], ga[:, c, :], chT[:, c, 40:41], None, ALU.mult).then_inc(s["ya_done"], 1)
            for t, (t0, n) in enumerate(TILES):
                def v3(ap):
                    return ap.rearrange("p (g d) -> p g d", g=8)
                sq = wnat[0:n, 0:4, :].rearrange("p g q -> p (g q)")
                bs = (bsT if t < 2 else bsS)[0:n, :].rearrange("p (g o) -> p g o", o=1).to_broadcast([n, 8, 64])
                st = 7 * t
                uu = us[0:n, t, :]
                dve.tensor_tensor(v3(sq), v3(tp_get(f"s{t}")[0:n, :]), bs, ALU.add).then_inc(s["tp_evac"], 1)
                dve.wait_ge(s["tp_evac"], TP[f"s{t}"] + 1)
                dve.wait_ge(s["prj_evac"], prj_no[("u", t)] + 1)
                if t == 2:
                    dve.wait_ge(s["gelu_half"], 2)
                dve.tensor_tensor(uu, uu, sq, ALU.mult).then_inc(s["yb_step"], 1)
                dve.wait_ge(s["yb_step"], st + 1)
                dve.tensor_tensor(sq, uu, uu, ALU.mult).then_inc(s["yb_step"], 1)
                dve.wait_ge(s["yb_step"], st + 2)
                gs = small[0:n, 16:24]
                dve.tensor_reduce(gs, v3(sq), AX, ALU.add).then_inc(s["yb_step"], 1)
                dve.wait_ge(s["yb_step"], st + 3)
                dve.tensor_scalar(gs, gs, 1.0 / 64, EPS, ALU.mult, ALU.add).then_inc(s["yb_step"], 1)
                dve.wait_ge(s["yb_step"], st + 4)
                dve.tensor_tensor(uu, uu, og_row[0:n, :], ALU.mult).then_inc(s["yb_step"], 1)
                dve.wait_ge(s["yb_step"], st + 5)
                dve.reciprocal(gs, gs).then_inc(s["yb_step"], 1)
                dve.wait_ge(s["yb_sqrt"], t + 1)
                dve.tensor_tensor(v3(uu), v3(uu), gs.rearrange("p (g o) -> p g o", o=1).to_broadcast([n, 8, 64]), ALU.mult).then_inc(s["yb_step"], 1)
            dve.memset(spare, 0.0).then_inc(s["mix_free"], 1)
            dve.wait_ge(s["gm_in"], 4)
            dve.wait_ge(s["prj_evac"], len(PRJ))
            scales("gn_ffn", 16)
            dve.wait_ge(s["mod_scaled"], 2)
            work = et[:, 4096 + HALF:4096 + HALF + D]

            def residual(t):
                n = TILES[t][1]
                for c in range(2):
                    q = min(2 * t + c, 4)
                    src = bank[WO_BANK[q]][0:n, :]
                    dve.wait_ge(s["wout_ready"], q + 1)
                    if 2 * t + c == 5:
                        dve.wait_ge(s["wo_moved"], 1)
                        src = wo_hi
                    wk = work[0:n, c * HALF:(c + 1) * HALF]
                    link(dve.tensor_tensor(wk, src, gmod[0:n, t // 2, c * HALF:(c + 1) * HALF], ALU.mult))
                    if c == 0:
                        link(dve.tensor_tensor(x[0:n, t, 0:HALF], x[0:n, t, 0:HALF], wk, ALU.add))
                    else:
                        dve.tensor_tensor(x[0:n, t, HALF:D], x[0:n, t, HALF:D], wk, ALU.add).then_inc(s["x2_done"], 1)

            def norm2(t):
                n = TILES[t][1]
                dve.wait_ge(s["x2_sq"], t + 1)
                dve.tensor_scalar(rstd[0:n, t:t + 1], ssq[0:n, t:t + 1], 1.0 / D, EPS, ALU.mult, ALU.add).then_inc(s["rs2_in"], 1)
                dve.wait_ge(s["rs2_in"], 2 * t + 1)
                dve.reciprocal(rstd[0:n, t:t + 1], rstd[0:n, t:t + 1]).then_inc(s["rs2_in"], 1)
                dve.wait_ge(s["rs2"], t + 1)
                if t == 0:
                    dve.wait_ge(s["v_out"], 16)
                normed(t, "xn_ready", work)
                dve.wait_ge(s["xn_ready"], t + 1)

            residual(0)
            dve.tensor_copy(hrow[0:36, :], tp_get("hc")[0:36, :]).then_inc(s["tp_evac"], 1)
            dve.wait_ge(s["tp_evac"], TP["hc"] + 1)
            dve.memset(spare, 0.0).then_inc(s["hc_done"], 1)
            norm2(0)
            residual(1)
            dve.wait_ge(s["x2_done"], 2)
            norm2(1)
            residual(2)
            dve.wait_ge(s["x2_done"], 3)
            norm2(2)
            dve.memset(score[64:P, 2, :], 0.5).then_inc(s["pad_set"], 1)
            dve.memset(pos[64:P, 2, :], 0.0).then_inc(s["pad_set"], 1)
            def over_e(ap):
                return ap.rearrange("p (t o) -> p t o", o=1).to_broadcast([P, 3, NE])
            link(dve.tensor_copy(tg[:, :, :, 0, 0], over_e(tokc[:, :])))
            link(dve.tensor_tensor(rsc[:, 3:6], tokc[:, :], tg[:, :, 0, 0, 0], ALU.subtract))
            dve.tensor_copy(tg[:, :, :, 0, 1], over_e(rsc[:, 3:6])).then_inc(s["code_in"], 1)
            dve.memset(tg[:, :, :, 0, 2], 0.0).then_inc(s["code_in"], 1)
            dve.wait_ge(s["code_in"], 2)
            dve.wait_ge(s["sc_done"], 3)
            dve.wait_ge(s["ld_router"], 32)
            link(dve.tensor_tensor(biased, score, rbias[:, :].rearrange("p (o e) -> p o e", o=1).to_broadcast([P, 3, NE]), ALU.add))
            for t in range(3):
                dve.max(top[:, t, :], biased[:, t, :]).then_inc(s["route_step"], 1)
            dve.wait_ge(s["route_step"], 3)
            for t in range(3):
                dve.match_replace(rest[:, t, :], top[:, t, :], biased[:, t, :], -3.0e38).then_inc(s["route_step"], 1)
            dve.wait_ge(s["route_step"], 6)
            dve.tensor_scalar(mask, rest, -3.0e38, None, ALU.is_equal).then_inc(s["mask_done"], 1)
            dve.wait_ge(s["mask_done"], 1)
            link(dve.tensor_tensor(score, score, mask, ALU.mult))
            link(dve.tensor_reduce(rsc[:, 0:3], score, AX, ALU.add))
            link(dve.reciprocal(rsc[:, 0:3], rsc[:, 0:3]))
            link(dve.tensor_scalar(rsc[:, 0:3], rsc[:, 0:3], 2.5, None, ALU.mult))
            link(dve.tensor_tensor(gpart, score, over_e(rsc[:, 0:3]), ALU.mult))
            link(dve.tensor_copy(tg[:, :, :, 1, 0], gpart))
            link(dve.tensor_tensor(gpart, gpart, tg[:, :, :, 1, 0], ALU.subtract))
            link(dve.tensor_copy(tg[:, :, :, 1, 1], gpart))
            link(dve.tensor_tensor(gpart, gpart, tg[:, :, :, 1, 1], ALU.subtract))
            dve.tensor_copy(tg[:, :, :, 1, 2], gpart).then_inc(s["route_step"], 1)
            b = tp_get("pos")
            for t, (t0, n) in enumerate(TILES):
                dve.scalar_tensor_tensor(pos[0:n, t, :], b[0:n, t * NE:(t + 1) * NE], 1.0, mask[0:n, t, :], ALU.add, ALU.mult).then_inc(s["route_step"], 1)
            dve.wait_ge(s["route_step"], 10)
            link(dve.tensor_scalar(pos, pos, -1.0, None, ALU.add))
            def counts():
                link(dve.tensor_reduce(cmax, b[:, 3 * NE:4 * NE], AX, ALU.max))
                link(dve.tensor_copy(cnt_i[:, NE:NE + 1], cmax))
                dve.tensor_copy(cnt_i[:, 0:NE], b[:, 3 * NE:4 * NE]).then_inc(s["tp_evac"], 1)
                dve.wait_ge(s["tp_evac"], TP["pos"] + 1)
                dve.memset(spare, 0.0).then_inc(s["flags"], 1)

            def shared_hidden(t):
                n = TILES[t][1]
                dve.wait_ge(s["sh_act"], t + 1)
                if t == 2:
                    dve.wait_ge(s["up_moved"], 1)
                if t:
                    dve.wait_ge(s["h_ready"], t)
                dve.tensor_tensor(shid[0:n, :].rearrange("t (j p) -> t p j", j=2), sgs[0:n, :].rearrange("t (p j) -> t p j", j=2),
                                  (bank[4 + t][0:n, FE:2 * FE] if t < 2 else up_s).rearrange("t (p j) -> t p j", j=2), ALU.mult).then_inc(s["sh_hid"], 1)

            def shared_turned(t):
                n = TILES[t][1]
                dve.wait_ge(s["h_ready"], t + 1)
                if t:
                    dve.wait_ge(s["sh_down_ready"], 2 * t)
                dve.tensor_copy(shT[:, :, 0:n], bank[4][:, 0:2 * P].rearrange("p (j n) -> p j n", j=2)[:, :, 0:n]).then_inc(s["h_evac"], 1)

            def select(r, i, u):
                e = r * NE + i * U + u
                if not (isinstance(e, int) and e == 0):
                    dve.wait_ge(s["sel_ready"], e)
                for t, (t0, n) in enumerate(TILES):
                    ins = dve.tensor_scalar(sel[0:n, t, :], iota_s[0:n, :], pos[0:n, t, bass.ds(i * U + u, 1)], None, ALU.is_equal)
                ins.then_inc(s["sel_built"], 1)

            def index(r, i, u):
                e = r * NE + i * U + u
                dve.wait_ge(s["sel_ready"], e + 1)
                if not (isinstance(e, int) and e < U):
                    for b in range(2):
                        dve.wait_ge(scattered[b], 16 * e - 16 * (U - 1))
                dve.tensor_reduce(pick_out[:, u], bank[7][:, 0:12].rearrange("p (b c m) -> p b c m", b=2, c=2), AX, ALU.add)\
                   .then_inc(s["gate_ready"], 1)
                dve.wait_ge(s["gate_ready"], e + 1)
                dve.tensor_scalar(idx[:, u, :], pick_out[:, u, :, 0], halfc[:, 0:1], None, ALU.add).then_inc(s["idx_ready"], 1)

            def xt0(r, i, u):
                dve.wait_ge(s["xt_ready"], r * NE + i * U + u + 1)
                dve.tensor_copy(xt[:, 0].rearrange("p k h n -> p (k h n)"), bank[2][:, :]).then_inc(s["xt0_evac"], 1)

            def hidden(r, i, u):
                e = r * NE + i * U + u
                dve.wait_ge(s["up_evac"], e + 1)
                if not (isinstance(e, int) and e == 0):
                    dve.wait_ge(s["ht_ready"], e)
                dve.tensor_tensor(hid[0:64].rearrange("t b j p -> t b p j"), sg[0:64, :].rearrange("t (b p j) -> t b p j", b=2, j=2),
                                  up[0:64, :].rearrange("t (b p j) -> t b p j", b=2, j=2), ALU.mult).then_inc(s["hid_ready"], 1)

            def ht(r, i, u):
                dve.wait_ge(s["ht_ready"], r * NE + i * U + u + 1)
                if not (isinstance(i, int) and i == 0 and u == 0 and r == 0):
                    dve.wait_ge(s["y_ready"], r * NE + i * U + u)
                dve.tensor_copy(hT.rearrange("p b j n -> p (b j n)"), bank[4][:, 0:256]).then_inc(s["ht_evac"], 1)

            def y0(r, i, u):
                e = r * NE + i * U + u
                dve.wait_ge(s["y_ready"], e + 1)
                if not (isinstance(e, int) and e < 2):
                    dve.wait_ge(scattered[0], 16 * e - 16)
                dve.tensor_scalar(yo[:, u % 2, 0, :], bank[5][:, :], pick_out[:, u, 0, 1:2], None, ALU.mult).then_inc(s["y0_evac"], 1)

            def body(r, i, first=False, last=False):
                for u in range(U):
                    before = (r, i if u else i - 1, (u - 1) % U)
                    if not (last and u >= U - 2):
                        select(r, i + (u + 2) // U, (u + 2) % U)
                    if not (first and u == 0):
                        ht(*before)
                    if not (last and u >= U - 2):
                        index(r, i + (u + 2) // U, (u + 2) % U)
                    if not (last and u == U - 1):
                        xt0(r, i + (u + 1) // U, (u + 1) % U)
                    if first and u == 0 and r == 0:
                        shared_turned(1)
                        shared_hidden(2)
                        shared_turned(2)
                    hidden(r, i, u)
                    if not (first and u == 0):
                        y0(*before)

            def rounds(r):
                if r == 0:
                    dve.wait_ge(s["iota_in"], 1)
                select(r, 0, 0)
                if r == 0:
                    counts()
                index(r, 0, 0)
                select(r, 0, 1)
                if r == 0:
                    shared_hidden(0)
                index(r, 0, 1)
                if r == 0:
                    shared_turned(0)
                    shared_hidden(1)
                xt0(r, 0, 0)
                body(r, 0, first=True)
                if r == 0:
                    dve.wait_ge(s["gf_in"], 8)
                    dve.wait_ge(s["sh_evac"], 6)
                    for t, (t0, n) in enumerate(TILES):
                        link(dve.tensor_tensor(sh[0:n, t, :], sh[0:n, t, :], gmod[0:n, t // 2, :], ALU.mult))
                        dve.tensor_tensor(x[0:n, t, :], x[0:n, t, :], sh[0:n, t, :], ALU.add).then_inc(s["pre_done"], 1)
                with dve.Fori(1, NE // U - 1) as i:
                    body(r, i)
                body(r, NE // U - 1, last=True)
                ht(r, NE // U - 1, U - 1)
                y0(r, NE // U - 1, U - 1)

            def out(t):
                n = TILES[t][1]
                turn = FIN_ORDER.index(t)
                dve.wait_ge(s["fin_rs"], 2 * turn + 1)
                dve.tensor_scalar(frs[0:n, t:t + 1], fss[0:n, t:t + 1], 1.0 / D, EPS, ALU.mult, ALU.add).then_inc(s["rs_in"], 1)
                dve.wait_ge(s["rs_in"], 4 + 2 * turn + 1)
                dve.reciprocal(frs[0:n, t:t + 1], frs[0:n, t:t + 1]).then_inc(s["rs_in"], 1)
                dve.wait_ge(s["fin_rs"], 2 * turn + 2)
                dve.scalar_tensor_tensor(xn[0:n, t, :], xn[0:n, t, :], frs[0:n, t:t + 1], gn[0:n, :], ALU.mult, ALU.mult).then_inc(s["out_done"], 1)

            rounds(0)
            most = dve.value_load(cnt_i[0:1, NE:NE + 1], min_val=0, max_val=T)
            for r in range(1, ROUNDS):
                with dve.If(most > r * ROUND):
                    for t, (t0, n) in enumerate(TILES):
                        dve.tensor_scalar(pos[0:n, t, :], pos[0:n, t, :], -float(ROUND), None, ALU.add).then_inc(s["pos_shifted"], 1)
                    dve.wait_ge(s["pos_shifted"], 3 * r)
                    rounds(r)
            dve.wait_ge(s["gn_fin"], 16)
            for t in range(2):
                w = xn[:, t, :]
                dve.wait_ge(acc_back[t], 32)
                dve.tensor_tensor(w, w, sh[:, t, :], ALU.add).then_inc(s["fin_sq"], 1)
                dve.wait_ge(s["fin_sq"], 3 * t + 1)
                dve.tensor_tensor(w, w, gmod[:, 0, :], ALU.mult).then_inc(s["fin_sq"], 1)
                dve.wait_ge(s["fin_sq"], 3 * t + 2)
                dve.tensor_tensor(w, w, x[:, t, :], ALU.add).then_inc(s["fin_sq"], 1)
                if t:
                    out(0)
            out(2)
            out(1)


_INS = ["x_prompt", "x_sample", "c_prompt", "c_sample", "state_lru_h", "state_conv", "ada_w", "ada_b", "norm_mix_g",
        "norm_ffn_g", "w_in", "conv_w", "conv_b", "gate_r_w", "gate_r_b", "gate_i_w", "gate_i_b", "lru_lambda",
        "sgu_norm_g", "sgu_w", "sgu_b", "out_norm_g", "w_out", "router_w", "router_bias", "exp_w_gate", "exp_w_up",
        "exp_w_down", "shared_w_gate", "shared_w_up", "shared_w_down", "final_norm_g"]
_OUTS = [("y_prompt", (1, NPR, D)), ("y_sample", (NB, NT, D)), ("h_prompt", (1, 1, W)), ("conv_prompt", (1, 1, CW - 1, W)),
         ("h_sample", (1, NB, W)), ("conv_sample", (1, NB, CW - 1, W)), ("v_sample", (1, NB, NT, W))]


def kernel(**inputs):
    import numpy as np
    import concourse.bacc as bacc
    from concourse.bass_utils import run_bass_kernel_spmd as run

    nc = bacc.Bacc("TRN2", target_bir_lowering=False, num_devices=1)
    arrays, io = {}, {}
    for name in _INS:
        a = np.ascontiguousarray(inputs[name])
        arrays[f"in_{name}"] = a
        io[name] = nc.dram_tensor(f"in_{name}", a.shape, mybir.dt.from_np(a.dtype), kind="ExternalInput").ap()
    for name, shape in _OUTS:
        io[name] = nc.dram_tensor(f"out_{name}", shape, F32, kind="ExternalOutput").ap()
    build(nc, io)
    r = run(nc, [arrays], core_ids=[0])
    return tuple(r.results[0][f"out_{name}"] for name, _ in _OUTS)
```
